# Optimizing a Trainium2 kernel written in Bass

```python
import math
import jax, jax.numpy as jnp
from jax import lax
import numpy as np

D_MODEL = 1024
BATCH = 1
SEQ = 256
DEPTH = 2

GRID_W = 64
CTX_LEN = 256
LN_EPS = 1e-5

HEAD_DIM = 64
N_HEADS_A = D_MODEL // (2 * HEAD_DIM)
V_DIM = 2 * HEAD_DIM
QK_W = N_HEADS_A * 2 * HEAD_DIM
V_W = N_HEADS_A * V_DIM
ATTN_OUT = V_W
ATTN_SCALE = HEAD_DIM ** -0.5
Q_BLOCK = 128
ROPE_BASE = 10000.0
ROPE_AXIS_PAIRS = HEAD_DIM // 4

CHUNK = 128
SGU_GROUPS = 4
SGU_W = D_MODEL // 2
SGU_GC = SGU_W // SGU_GROUPS

AB_IN = 2 * QK_W + V_W + 2 * SGU_W
AB_OUT = ATTN_OUT + SGU_W
AB_SPLITS = [QK_W, 2 * QK_W, 2 * QK_W + V_W, 2 * QK_W + V_W + SGU_W]

POOL_WINDOWS = (2, 4, 8, 16)
N_POOL_GROUPS = len(POOL_WINDOWS)
POOL_W = D_MODEL
POOL_GC = POOL_W // N_POOL_GROUPS

P_HEADS = 8
N_KEYS = 128
N_EXPERTS = N_KEYS * N_KEYS
P_TOPK = 16
D_KEY = 256
D_KEY_HALF = D_KEY // 2
PEER_BLOCK = 128


def layer_norm(h, g, b):
    h32 = h.astype(jnp.float32)
    mu = jnp.mean(h32, axis=-1, keepdims=True)
    var = jnp.mean(jnp.square(h32 - mu), axis=-1, keepdims=True)
    out = (h32 - mu) * lax.rsqrt(var + LN_EPS) * g.astype(jnp.float32) + b.astype(jnp.float32)
    return out.astype(h.dtype)

def modulate(h, shift, scale):
    return h * (1.0 + scale) + shift

def axial_rope_tables(rows):
    row = jnp.repeat(jnp.arange(rows, dtype=jnp.float32), GRID_W)
    col = jnp.tile(jnp.arange(GRID_W, dtype=jnp.float32), rows)
    inv = ROPE_BASE ** (-jnp.arange(ROPE_AXIS_PAIRS, dtype=jnp.float32) / ROPE_AXIS_PAIRS)
    ang = jnp.concatenate([row[:, None] * inv, col[:, None] * inv], axis=-1)
    return jnp.cos(ang), jnp.sin(ang)

def apply_rope(t, cos, sin):
    t32 = t.astype(jnp.float32)
    half = HEAD_DIM // 2
    a, b = t32[..., :half], t32[..., half:]
    cs = cos[None, :, None, None, :]
    sn = sin[None, :, None, None, :]
    return jnp.concatenate([a * cs - b * sn, a * sn + b * cs], axis=-1).astype(t.dtype)

def diff_attn_block(q, k, v, lam):
    s = jnp.einsum('bqhmd,bkhmd->bhmqk', q, k).astype(jnp.float32) * ATTN_SCALE
    p = jax.nn.softmax(s, axis=-1)
    a = (p[:, :, 0] - lam * p[:, :, 1]).astype(v.dtype)
    return jnp.einsum('bhqk,bkhe->bqhe', a, v)

def head_rms(o, g, lam_init):
    o32 = o.astype(jnp.float32)
    o32 = o32 * lax.rsqrt(jnp.mean(o32 * o32, axis=-1, keepdims=True) + LN_EPS)
    return (o32 * g.astype(jnp.float32) * (1.0 - lam_init)).astype(o.dtype)

def spatial_gate(gu, gv, ln_g, ln_b, w_s, b_s):
    u = jax.nn.gelu(gu)
    v = layer_norm(jax.nn.gelu(gv), ln_g, ln_b)
    bsz, t, _ = v.shape
    v = v.reshape(bsz, t // CHUNK, CHUNK, SGU_GROUPS, SGU_GC)
    s = jnp.einsum('gpq,bnqgc->bnpgc', w_s, v) + b_s.T[:, :, None]
    return u * s.reshape(bsz, t, SGU_W)

def mixer_ab(hx, hc, w_in, w_out, lam_vec, norm_g, sgu_ln_g, sgu_ln_b, sgu_w, sgu_b,
             lam_init, cos, sin, ctx_out):
    bsz, s_len, _ = hx.shape
    c_len = hc.shape[1]
    lq1, lk1, lq2, lk2 = lam_vec.astype(jnp.float32)
    lam = jnp.exp(jnp.sum(lq1 * lk1)) - jnp.exp(jnp.sum(lq2 * lk2)) + lam_init
    q_x, k_x, v_x, gu_x, gv_x = jnp.split(hx @ w_in, AB_SPLITS, axis=-1)
    q_x = apply_rope(q_x.reshape(bsz, s_len, N_HEADS_A, 2, HEAD_DIM), cos, sin)
    k_x = apply_rope(k_x.reshape(bsz, s_len, N_HEADS_A, 2, HEAD_DIM), cos, sin)
    v_x = v_x.reshape(bsz, s_len, N_HEADS_A, V_DIM)
    if ctx_out:
        q_c, k_c, v_c, gu_c, gv_c = jnp.split(hc @ w_in, AB_SPLITS, axis=-1)
    else:
        k_c, v_c = jnp.split(hc @ w_in[:, QK_W:2 * QK_W + V_W], [QK_W], axis=-1)
    k_c = k_c.reshape(bsz, c_len, N_HEADS_A, 2, HEAD_DIM)
    v_c = v_c.reshape(bsz, c_len, N_HEADS_A, V_DIM)
    k_all = jnp.concatenate([k_c, k_x], axis=1)
    v_all = jnp.concatenate([v_c, v_x], axis=1)
    n_blk = s_len // Q_BLOCK
    qb = jnp.moveaxis(q_x.reshape(bsz, n_blk, Q_BLOCK, N_HEADS_A, 2, HEAD_DIM), 1, 0)
    o_x = lax.map(lambda qblk: diff_attn_block(qblk, k_all, v_all, lam), qb)
    o_x = jnp.moveaxis(o_x, 0, 1).reshape(bsz, s_len, N_HEADS_A, V_DIM)
    a_x = head_rms(o_x, norm_g, lam_init).reshape(bsz, s_len, ATTN_OUT)
    g_x = spatial_gate(gu_x, gv_x, sgu_ln_g, sgu_ln_b, sgu_w, sgu_b)
    y_x = jnp.concatenate([a_x, g_x], axis=-1) @ w_out
    if not ctx_out:
        return y_x, None
    q_c = q_c.reshape(bsz, c_len, N_HEADS_A, 2, HEAD_DIM)
    o_c = diff_attn_block(q_c, k_c, v_c, lam)
    a_c = head_rms(o_c, norm_g, lam_init).reshape(bsz, c_len, ATTN_OUT)
    g_c = spatial_gate(gu_c, gv_c, sgu_ln_g, sgu_ln_b, sgu_w, sgu_b)
    y_c = jnp.concatenate([a_c, g_c], axis=-1) @ w_out
    return y_x, y_c

def multiscale_pool(h):
    bsz, t, _ = h.shape
    h32 = h.astype(jnp.float32)
    cs = jnp.concatenate([jnp.zeros((bsz, 1, POOL_W), jnp.float32), jnp.cumsum(h32, axis=1)], axis=1)
    pos = jnp.arange(t)
    outs = []
    for g, w in enumerate(POOL_WINDOWS):
        lo = jnp.clip(pos - w // 2, 0, t)
        hi = jnp.clip(pos + (w - w // 2), 0, t)
        seg = cs[:, :, g * POOL_GC:(g + 1) * POOL_GC]
        cnt = (hi - lo).astype(jnp.float32)[None, :, None]
        outs.append((seg[:, hi] - seg[:, lo]) / cnt)
    pooled = jnp.concatenate(outs, axis=-1)
    return (pooled - h32).astype(h.dtype)

def mixer_pool(h, w_in, w_grp, scale, w_out):
    m = multiscale_pool(h @ w_in)
    bsz, t, _ = m.shape
    m = jnp.einsum('btgc,gce->btge', m.reshape(bsz, t, N_POOL_GROUPS, POOL_GC), w_grp)
    return (m.reshape(bsz, t, POOL_W) * scale) @ w_out

def peer(h, wq, keys, u_tab, v_tab):
    n, d = h.shape
    hb = h.reshape(n // PEER_BLOCK, PEER_BLOCK, d)

    def block(hblk):
        q = (hblk @ wq).reshape(PEER_BLOCK, P_HEADS, 2, D_KEY_HALF)
        s = jnp.einsum('nhpd,hpkd->nhpk', q, keys).astype(jnp.float32)
        top_s, top_i = lax.top_k(s, P_TOPK)
        cand_s = (top_s[:, :, 0, :, None] + top_s[:, :, 1, None, :]).reshape(PEER_BLOCK, P_HEADS, P_TOPK * P_TOPK)
        cand_i = (top_i[:, :, 0, :, None] * N_KEYS + top_i[:, :, 1, None, :]).reshape(PEER_BLOCK, P_HEADS, P_TOPK * P_TOPK)
        best_s, best_pos = lax.top_k(cand_s, P_TOPK)
        idx = jnp.take_along_axis(cand_i, best_pos, axis=-1)
        gate = jax.nn.softmax(best_s, axis=-1)
        u = u_tab[idx]
        v = v_tab[idx]
        act = jax.nn.gelu(jnp.einsum('nd,nhkd->nhk', hblk, u))
        return jnp.einsum('nhk,nhkd->nd', (gate * act).astype(v.dtype), v)

    return lax.map(block, hb).reshape(n, d)

def first_inputs(seed: int = 0) -> dict:
    key = jax.random.key(seed)
    ks = jax.random.split(key, 24)
    n_even = (DEPTH + 1) // 2
    n_odd = DEPTH // 2
    beta = (8.0 * DEPTH) ** -0.25

    def nrm(k, shape, s):
        return jax.random.normal(k, shape, jnp.float32) * s

    return {
        'x': nrm(ks[0], (BATCH, SEQ, D_MODEL), 1.0),
        'c': nrm(ks[1], (BATCH, D_MODEL), 1.0),
        'ctx': nrm(ks[2], (BATCH, CTX_LEN, D_MODEL), 1.0),
        'c_ctx': nrm(ks[3], (D_MODEL,), 1.0),
        'ada_w': nrm(ks[4], (DEPTH, D_MODEL, 6 * D_MODEL), 0.5 * D_MODEL ** -0.5),
        'ada_b': nrm(ks[5], (DEPTH, 6 * D_MODEL), 0.02),
        'ln_g': 1.0 + nrm(ks[6], (DEPTH, 2, D_MODEL), 0.05),
        'ln_b': nrm(ks[7], (DEPTH, 2, D_MODEL), 0.02),
        'ab_w_in': nrm(ks[8], (n_even, D_MODEL, AB_IN), D_MODEL ** -0.5),
        'ab_w_out': nrm(ks[9], (n_even, AB_OUT, D_MODEL), beta * AB_OUT ** -0.5),
        'diff_lam': nrm(ks[10], (n_even, 4, HEAD_DIM), 0.1),
        'diff_norm_g': 1.0 + nrm(ks[11], (n_even, V_DIM), 0.05),
        'sgu_ln_g': 1.0 + nrm(ks[12], (n_even, SGU_W), 0.05),
        'sgu_ln_b': nrm(ks[13], (n_even, SGU_W), 0.02),
        'sgu_w': nrm(ks[14], (n_even, SGU_GROUPS, CHUNK, CHUNK), CHUNK ** -0.5),
        'sgu_b': 1.0 + nrm(ks[15], (n_even, SGU_GROUPS, CHUNK), 0.1),
        'pool_w_in': nrm(ks[16], (n_odd, D_MODEL, POOL_W), D_MODEL ** -0.5),
        'pool_w_grp': nrm(ks[17], (n_odd, N_POOL_GROUPS, POOL_GC, POOL_GC), POOL_GC ** -0.5),
        'pool_scale': 1.0 + nrm(ks[18], (n_odd, POOL_W), 0.1),
        'pool_w_out': nrm(ks[19], (n_odd, POOL_W, D_MODEL), beta * POOL_W ** -0.5),
        'peer_wq': nrm(ks[20], (DEPTH, D_MODEL, P_HEADS * D_KEY), D_MODEL ** -0.5),
        'peer_keys': nrm(ks[21], (DEPTH, P_HEADS, 2, N_KEYS, D_KEY_HALF), D_KEY_HALF ** -0.5),
        'peer_u': nrm(ks[22], (DEPTH, N_EXPERTS, D_MODEL), D_MODEL ** -0.5),
        'peer_v': nrm(ks[23], (DEPTH, N_EXPERTS, D_MODEL), beta),
    }

def first_block(x, c, ctx, c_ctx, ada_w, ada_b, ln_g, ln_b, ab_w_in, ab_w_out, diff_lam,
              diff_norm_g, sgu_ln_g, sgu_ln_b, sgu_w, sgu_b, pool_w_in, pool_w_grp,
              pool_scale, pool_w_out, peer_wq, peer_keys, peer_u, peer_v):
    bsz, s_len, d = x.shape
    c_len = ctx.shape[1]
    rows = s_len // GRID_W
    cos, sin = axial_rope_tables(rows)
    alpha = (2.0 * DEPTH) ** 0.25
    last_ctx_read = 2 * ((DEPTH - 1) // 2)
    silu_c = jax.nn.silu(c)
    silu_cc = jax.nn.silu(c_ctx)
    xs, cs = x, ctx
    for i in range(DEPTH):
        j = i // 2
        even = i % 2 == 0
        ctx_out = i < last_ctx_read
        sh1, sc1, g1, sh2, sc2, g2 = jnp.split((silu_c @ ada_w[i] + ada_b[i])[:, None, :], 6, axis=-1)
        hx = modulate(xs, sh1, sc1)
        if ctx_out or even:
            csh1, csc1, cg1, csh2, csc2, cg2 = jnp.split(silu_cc @ ada_w[i] + ada_b[i], 6, axis=-1)
            hc = modulate(cs, csh1, csc1)
        if even:
            lam_init = 0.8 - 0.6 * math.exp(-0.3 * i)
            yx, yc = mixer_ab(hx, hc, ab_w_in[j], ab_w_out[j], diff_lam[j], diff_norm_g[j],
                              sgu_ln_g[j], sgu_ln_b[j], sgu_w[j], sgu_b[j], lam_init, cos, sin, ctx_out)
        else:
            yx = mixer_pool(hx, pool_w_in[j], pool_w_grp[j], pool_scale[j], pool_w_out[j])
            yc = mixer_pool(hc, pool_w_in[j], pool_w_grp[j], pool_scale[j], pool_w_out[j]) if ctx_out else None
        xs = layer_norm(alpha * xs + g1 * yx, ln_g[i, 0], ln_b[i, 0])
        hx = modulate(xs, sh2, sc2)
        if ctx_out:
            cs = layer_norm(alpha * cs + cg1 * yc, ln_g[i, 0], ln_b[i, 0])
            hc = modulate(cs, csh2, csc2)
            f = peer(jnp.concatenate([hc, hx], axis=1).reshape(-1, d),
                     peer_wq[i], peer_keys[i], peer_u[i], peer_v[i]).reshape(bsz, c_len + s_len, d)
            fc, fx = f[:, :c_len], f[:, c_len:]
            cs = layer_norm(alpha * cs + cg2 * fc, ln_g[i, 1], ln_b[i, 1])
        else:
            fx = peer(hx.reshape(-1, d), peer_wq[i], peer_keys[i], peer_u[i], peer_v[i]).reshape(bsz, s_len, d)
        xs = layer_norm(alpha * xs + g2 * fx, ln_g[i, 1], ln_b[i, 1])
    return xs


N_MIXERS = 2
N_MOBA = (DEPTH + 1) // 2
N_GDN = DEPTH // 2

MOBA_HEAD_DIM = 128
MOBA_HEADS = D_MODEL // MOBA_HEAD_DIM
MOBA_WIDTH = MOBA_HEADS * MOBA_HEAD_DIM
MOBA_BLOCK = 256
MOBA_TOP_K = 3
MOBA_Q_CHUNK = 64
MOBA_IN = 4 * MOBA_WIDTH

GDN_HEAD_DIM = 128
GDN_HEADS = D_MODEL // GDN_HEAD_DIM
GDN_WIDTH = GDN_HEADS * GDN_HEAD_DIM
GDN_CONV = 4
GDN_CHUNK = 64
GDN_IN = 4 * GDN_WIDTH + 2 * GDN_HEADS

DEEPNORM_ALPHA = (2.0 * DEPTH) ** 0.25
DEEPNORM_BETA = (8.0 * DEPTH) ** -0.25
RMS_EPS = 1e-6
L2_EPS = 1e-6
ADA_INIT_SCALE = 0.1
NEG = -1e30


def layer_norm_2(x, g, b):
    xf = x.astype(jnp.float32)
    mu = jnp.mean(xf, axis=-1, keepdims=True)
    var = jnp.mean(jnp.square(xf - mu), axis=-1, keepdims=True)
    y = (xf - mu) * lax.rsqrt(var + LN_EPS)
    return (y * g.astype(jnp.float32) + b.astype(jnp.float32)).astype(x.dtype)

def l2_normalize(x):
    return x * lax.rsqrt(jnp.sum(jnp.square(x), axis=-1, keepdims=True) + L2_EPS)

def causal_depthwise_conv(u, w):
    k_w, ch = w.shape
    return lax.conv_general_dilated(
        u, w[:, None, :], window_strides=(1,), padding=[(k_w - 1, 0)],
        dimension_numbers=('NWC', 'WIO', 'NWC'), feature_group_count=ch)

def moba_attention(q, k, v):
    B, S, H, Dh = q.shape
    L = MOBA_BLOCK
    nb = -(-S // L)
    s_pad = nb * L
    pad = [(0, 0), (0, s_pad - S), (0, 0), (0, 0)]
    qh = jnp.pad(q, pad).transpose(0, 2, 1, 3)
    kb = jnp.pad(k, pad).transpose(0, 2, 1, 3).reshape(B, H, nb, L, Dh)
    vb = jnp.pad(v, pad).transpose(0, 2, 1, 3).reshape(B, H, nb, L, Dh)

    k_mean = jnp.mean(kb.astype(jnp.float32), axis=3)
    gate = jnp.einsum('bhsd,bhnd->bhsn', qh.astype(jnp.float32), k_mean)
    q_blk = jnp.arange(s_pad) // L
    cand = jnp.arange(nb)[None, :] < q_blk[:, None]
    gate = jnp.where(cand, gate, NEG)
    n_sel = max(1, min(MOBA_TOP_K, nb - 1))
    _, sel = lax.top_k(gate, n_sel)
    sel_valid = sel < q_blk[:, None]

    qc_n = MOBA_Q_CHUNK
    nqc = s_pad // qc_n
    cpb = L // qc_n

    def to_items(a):
        rest = a.shape[3:]
        a = jnp.moveaxis(a.reshape(B, H, nqc, qc_n, *rest), 2, 1)
        return a.reshape(B * nqc, H, qc_n, *rest)

    b_ids = jnp.repeat(jnp.arange(B, dtype=jnp.int32), nqc)
    c_ids = jnp.tile(jnp.arange(nqc, dtype=jnp.int32), B)
    scale = MOBA_HEAD_DIM ** -0.5
    h_idx = jnp.arange(H)[:, None, None]

    def attend(item):
        qc, selc, validc, b, ci = item
        kbb = kb[b]
        vbb = vb[b]
        kg = kbb[h_idx, selc]
        vg = vbb[h_idx, selc]
        blk = ci // cpb
        k_own = lax.dynamic_index_in_dim(kbb, blk, axis=1, keepdims=False)
        v_own = lax.dynamic_index_in_dim(vbb, blk, axis=1, keepdims=False)
        s_sel = jnp.einsum('hqd,hqnld->hqnl', qc, kg).astype(jnp.float32) * scale
        s_sel = jnp.where(validc[..., None], s_sel, NEG)
        s_own = jnp.einsum('hqd,hld->hql', qc, k_own).astype(jnp.float32) * scale
        q_pos = (ci % cpb) * qc_n + jnp.arange(qc_n)
        causal = jnp.arange(L)[None, :] <= q_pos[:, None]
        s_own = jnp.where(causal, s_own, NEG)
        s_all = jnp.concatenate([s_sel.reshape(H, qc_n, n_sel * L), s_own], axis=-1)
        p = jax.nn.softmax(s_all, axis=-1).astype(v.dtype)
        p_sel = p[..., :n_sel * L].reshape(H, qc_n, n_sel, L)
        p_own = p[..., n_sel * L:]
        return (jnp.einsum('hqnl,hqnld->hqd', p_sel, vg)
                + jnp.einsum('hql,hld->hqd', p_own, v_own))

    out = lax.map(attend, (to_items(qh), to_items(sel), to_items(sel_valid), b_ids, c_ids))
    out = out.reshape(B, nqc, H, qc_n, Dh).transpose(0, 1, 3, 2, 4).reshape(B, s_pad, H, Dh)
    return out[:, :S]

def chunk_gated_delta_rule(q, k, v, g, beta):
    B, S, H, Dk = q.shape
    Dv = v.shape[-1]
    C = GDN_CHUNK
    n = S // C

    def blk(a):
        return jnp.moveaxis(a.reshape(B, n, C, H, *a.shape[3:]), 3, 1)

    q = blk(q * (Dk ** -0.5))
    k = blk(k)
    v = blk(v)
    g = blk(g)
    beta = blk(beta)
    g_cum = jnp.cumsum(g, axis=-1)
    idx = jnp.arange(C)
    incl = idx[:, None] >= idx[None, :]
    strict = idx[:, None] > idx[None, :]
    diff = g_cum[..., :, None] - g_cum[..., None, :]
    decay_incl = jnp.exp(jnp.where(incl, diff, NEG))
    decay_strict = jnp.where(strict, decay_incl, 0.0)

    k_beta = k * beta[..., None]
    lmat = jnp.einsum('bhncd,bhnjd->bhncj', k_beta, k) * decay_strict
    a_mat = lmat + jnp.eye(C, dtype=lmat.dtype)
    rhs = jnp.concatenate([v * beta[..., None], k_beta * jnp.exp(g_cum)[..., None]], axis=-1)
    sol = lax.linalg.triangular_solve(a_mat, rhs, left_side=True, lower=True, unit_diagonal=True)
    u = sol[..., :Dv]
    w = sol[..., Dv:]
    a_qk = jnp.einsum('bhncd,bhnjd->bhncj', q, k) * decay_incl

    xs = tuple(jnp.moveaxis(t, 2, 0) for t in (q, k, u, w, g_cum, a_qk))

    def step(state, inp):
        qi, ki, ui, wi, gi, aqk = inp
        v_new = ui - jnp.einsum('bhcd,bhde->bhce', wi, state)
        o = (jnp.einsum('bhcd,bhde->bhce', qi * jnp.exp(gi)[..., None], state)
             + jnp.einsum('bhcj,bhje->bhce', aqk, v_new))
        g_last = gi[..., -1]
        k_dec = ki * jnp.exp(g_last[..., None] - gi)[..., None]
        state = state * jnp.exp(g_last)[..., None, None] + jnp.einsum('bhcd,bhce->bhde', k_dec, v_new)
        return state, o

    s0 = jnp.zeros((B, H, Dk, Dv), jnp.float32)
    _, o = lax.scan(step, s0, xs)
    o = jnp.moveaxis(o, 0, 2)
    return jnp.moveaxis(o, 1, 3).reshape(B, S, H, Dv)

def moba_branch(h, w_in, w_out):
    B, S, _ = h.shape
    proj = h @ w_in
    q, k, v, z = jnp.split(proj, [MOBA_WIDTH, 2 * MOBA_WIDTH, 3 * MOBA_WIDTH], axis=-1)
    shp = (B, S, MOBA_HEADS, MOBA_HEAD_DIM)
    o = moba_attention(q.reshape(shp), k.reshape(shp), v.reshape(shp))
    o = o.reshape(B, S, MOBA_WIDTH) * jax.nn.silu(z)
    return o @ w_out

def gdn_branch(h, w_in, conv_w, a_log, dt_bias, norm_w, w_out):
    B, S, _ = h.shape
    W = GDN_WIDTH
    proj = h @ w_in
    qkv = proj[..., :3 * W].astype(jnp.float32)
    z = proj[..., 3 * W:4 * W].astype(jnp.float32)
    a = proj[..., 4 * W:4 * W + GDN_HEADS].astype(jnp.float32)
    bt = proj[..., 4 * W + GDN_HEADS:].astype(jnp.float32)
    qkv = jax.nn.silu(causal_depthwise_conv(qkv, conv_w.astype(jnp.float32)))
    shp = (B, S, GDN_HEADS, GDN_HEAD_DIM)
    q = l2_normalize(qkv[..., :W].reshape(shp))
    k = l2_normalize(qkv[..., W:2 * W].reshape(shp))
    v = qkv[..., 2 * W:].reshape(shp)
    g = -jnp.exp(a_log.astype(jnp.float32)) * jax.nn.softplus(a + dt_bias.astype(jnp.float32))
    beta = jax.nn.sigmoid(bt)
    o = chunk_gated_delta_rule(q, k, v, g, beta)
    o = o * lax.rsqrt(jnp.mean(jnp.square(o), axis=-1, keepdims=True) + RMS_EPS)
    o = o * norm_w.astype(jnp.float32) * jax.nn.silu(z.reshape(shp))
    return o.reshape(B, S, W).astype(h.dtype) @ w_out

def second_inputs(seed: int = 0) -> dict:
    key = jax.random.key(seed)
    ks = jax.random.split(key, 16)
    f32 = jnp.float32
    x = jax.random.normal(ks[0], (BATCH, SEQ, D_MODEL), f32)
    c = jax.random.normal(ks[1], (BATCH, D_MODEL), f32)
    ada_w = jax.random.normal(ks[2], (DEPTH, D_MODEL, 3 * D_MODEL), f32) * (ADA_INIT_SCALE * D_MODEL ** -0.5)
    ada_base = jnp.concatenate([jnp.zeros((2 * D_MODEL,), f32), jnp.ones((D_MODEL,), f32)])
    ada_b = ada_base[None, :] + 0.01 * jax.random.normal(ks[3], (DEPTH, 3 * D_MODEL), f32)
    ln_g = 1.0 + 0.01 * jax.random.normal(ks[4], (DEPTH, D_MODEL), f32)
    ln_b = 0.01 * jax.random.normal(ks[5], (DEPTH, D_MODEL), f32)
    moba_w_in = jax.random.normal(ks[6], (N_MOBA, D_MODEL, MOBA_IN), f32) * D_MODEL ** -0.5
    moba_w_out = jax.random.normal(ks[7], (N_MOBA, MOBA_WIDTH, D_MODEL), f32) * (MOBA_WIDTH ** -0.5 * DEEPNORM_BETA)
    gdn_w_in = jax.random.normal(ks[8], (N_GDN, D_MODEL, GDN_IN), f32) * D_MODEL ** -0.5
    gdn_conv_w = jax.random.normal(ks[9], (N_GDN, GDN_CONV, 3 * GDN_WIDTH), f32) * GDN_CONV ** -0.5
    gdn_a_log = jnp.log(jax.random.uniform(ks[10], (N_GDN, GDN_HEADS), f32, 1.0, 16.0))
    dt = jnp.exp(jax.random.uniform(ks[11], (N_GDN, GDN_HEADS), f32, math.log(1e-3), math.log(1e-1)))
    gdn_dt_bias = dt + jnp.log(-jnp.expm1(-dt))
    gdn_norm_w = 1.0 + 0.01 * jax.random.normal(ks[12], (N_GDN, GDN_HEAD_DIM), f32)
    gdn_w_out = jax.random.normal(ks[13], (N_GDN, GDN_WIDTH, D_MODEL), f32) * (GDN_WIDTH ** -0.5 * DEEPNORM_BETA)
    return {"x": x, "c": c, "ada_w": ada_w, "ada_b": ada_b, "ln_g": ln_g, "ln_b": ln_b,
            "moba_w_in": moba_w_in, "moba_w_out": moba_w_out,
            "gdn_w_in": gdn_w_in, "gdn_conv_w": gdn_conv_w, "gdn_a_log": gdn_a_log,
            "gdn_dt_bias": gdn_dt_bias, "gdn_norm_w": gdn_norm_w, "gdn_w_out": gdn_w_out}

def second_block(x, c, ada_w, ada_b, ln_g, ln_b, moba_w_in, moba_w_out,
              gdn_w_in, gdn_conv_w, gdn_a_log, gdn_dt_bias, gdn_norm_w, gdn_w_out):
    cs = jax.nn.silu(c)
    for i in range(DEPTH):
        mod = cs @ ada_w[i] + ada_b[i]
        shift, scale, gate = jnp.split(mod, 3, axis=-1)
        h = x * (1.0 + scale[:, None, :]) + shift[:, None, :]
        j = i // N_MIXERS
        if i % N_MIXERS == 0:
            y = moba_branch(h, moba_w_in[j], moba_w_out[j])
        else:
            y = gdn_branch(h, gdn_w_in[j], gdn_conv_w[j], gdn_a_log[j], gdn_dt_bias[j],
                           gdn_norm_w[j], gdn_w_out[j])
        x = layer_norm_2(DEEPNORM_ALPHA * x + gate[:, None, :] * y, ln_g[i], ln_b[i])
    return x


def setup_inputs(seed=0):
    out = dict(first_inputs(seed))
    for name, value in second_inputs(seed + 1).items():
        if name != "x":
            out[name + "_2"] = value
    return out


def reference(
    x, c, ctx, c_ctx, ada_w, ada_b, ln_g, ln_b, ab_w_in, ab_w_out, diff_lam, diff_norm_g,
    sgu_ln_g, sgu_ln_b, sgu_w, sgu_b, pool_w_in, pool_w_grp, pool_scale, pool_w_out, peer_wq,
    peer_keys, peer_u, peer_v, c_2, ada_w_2, ada_b_2, ln_g_2, ln_b_2, moba_w_in_2, moba_w_out_2,
    gdn_w_in_2, gdn_conv_w_2, gdn_a_log_2, gdn_dt_bias_2, gdn_norm_w_2, gdn_w_out_2,
):
    x = first_block(
        x, c, ctx, c_ctx, ada_w, ada_b, ln_g, ln_b, ab_w_in, ab_w_out, diff_lam, diff_norm_g,
        sgu_ln_g, sgu_ln_b, sgu_w, sgu_b, pool_w_in, pool_w_grp, pool_scale, pool_w_out,
        peer_wq, peer_keys, peer_u, peer_v,
    )
    return second_block(
        x, c_2, ada_w_2, ada_b_2, ln_g_2, ln_b_2, moba_w_in_2, moba_w_out_2, gdn_w_in_2,
        gdn_conv_w_2, gdn_a_log_2, gdn_dt_bias_2, gdn_norm_w_2, gdn_w_out_2,
    )


_drawn_inputs = setup_inputs


def setup_inputs(seed=0):
    import zlib

    import numpy as np

    out = dict(_drawn_inputs(seed))
    spreads = {}
    factors = {'ada_b': 2.736,
     'diff_lam': 5.426,
     'diff_norm_g': 7.489,
     'sgu_ln_g': 8.0,
     'sgu_ln_b': 29.767,
     'sgu_b': 7.094,
     'pool_scale': 4.979,
     'ln_g_2': 11.692,
     'ln_b_2': 12.06,
     'gdn_norm_w_2': 49.764}
    for name, (base, spread) in spreads.items():
        noise = np.random.default_rng([zlib.crc32(name.encode()), seed]).standard_normal(out[name].shape)
        drawn = base * np.exp(spread * noise) if base else spread * noise
        out[name] = __import__('jax').numpy.asarray(drawn.astype(out[name].dtype))
    for name, factor in factors.items():
        out[name] = (out[name] * factor).astype(out[name].dtype)
    return out
```

```python
import math
import numpy as np
import concourse.bass as bass
from concourse import mybir

F = mybir.dt.float32
U32 = mybir.dt.uint32
ALU = mybir.AluOpType
ACT = mybir.ActivationFunctionType
AX = mybir.AxisListType.X
NEG = -1e30
ALPHA = 4.0 ** 0.25
RING = 6
NPART = 2
PW = 128 // NPART

CONST_AT = {}


def constants():
    p = np.arange(128)
    cols = []

    def put(name, a):
        CONST_AT[name] = (sum(x.shape[1] for x in cols), a.shape[1])
        cols.append(a.astype(np.float32))

    eye = np.eye(128)
    put("ident", eye)
    put("ones", np.ones((128, 128)))
    put("iota", np.broadcast_to(p[None, :], (128, 128)))
    put("iota16", np.broadcast_to(np.arange(16)[None, :], (128, 16)))
    put("persist_end", np.zeros((128, 0)))
    t = np.arange(256)
    inv = 10000.0 ** (-np.arange(16, dtype=np.float32) / 16)
    ang = np.concatenate([(t // 64)[:, None] * inv, (t % 64)[:, None] * inv], -1).astype(np.float32)
    put("cos", np.cos(ang).T[p % 32])
    put("sin", np.sin(ang).T[p % 32])
    perm = np.zeros((128, 128))
    for m in range(128):
        if m % 64 < 32:
            perm[m + 32, m] = -1.0
        else:
            perm[m - 32, m] = 1.0
    put("perm", perm)
    put("rope_end", np.zeros((128, 0)))
    pool = np.zeros((2, 128, 4, 256))
    for g, w in enumerate((2, 4, 8, 16)):
        for q in range(256):
            lo, hi = max(q - w // 2, 0), min(q + w - w // 2, 256)
            for s in range(lo, hi):
                pool[s // 128, s % 128, g, q] += 1.0 / (hi - lo)
            pool[q // 128, q % 128, g, q] -= 1.0
    put("pool", pool.transpose(1, 0, 2, 3).reshape(128, 2048))
    i, j = p[:, None], p[None, :]
    put("causal", np.where(j <= i, 0.0, NEG))
    put("utri", (i <= j) * 1.0)
    put("mD", np.where(j > i, -NEG, 0.0))
    put("mDT", np.where(j < i, NEG, 0.0))
    for b in (1, 2, 4, 8, 16, 32, 64):
        m = (i // (2 * b) == j // (2 * b)) & (i % (2 * b) >= b) & (j % (2 * b) < b)
        if b == 1:
            put("m1", m * 1.0)
        put(f"mt{b}", m.T * 1.0)
    put("gdn_end", np.zeros((128, 0)))
    return np.ascontiguousarray(np.concatenate(cols, 1))


PRM = [("c", 8), ("cc", 8), ("c2", 8), ("ab0", 48), ("ab1", 48), ("a20", 24), ("a21", 24),
       ("sgub", 4), ("psc", 8), ("conv", 96)]
ROWS = [("lam", 256), ("dng", 128), ("sg", 512), ("sb", 512), ("alog", 8), ("dt", 8), ("nw", 128)]


def offsets(table):
    at, out = 0, {}
    for name, w in table:
        out[name] = (at, w)
        at += w
    return out, at


PRM_AT, PRM_N = offsets(PRM)
ROW_AT, ROW_N = offsets(ROWS)

STREAM = ([("ada0", n) for n in range(24)] + [("abin", n) for n in range(16)]
          + [("about", n) for n in range(6)] + [("wq0", n) for n in range(8)] + [("keys0", 0)]
          + [("ada1", n) for n in range(24)] + [("uv0", n) for n in range(128)]
          + [("pin", n) for n in range(4)] + [("pgrp", 0)] + [("pout", n) for n in range(4)]
          + [("wq1", n) for n in range(8)] + [("keys1", 0)]
          + [("ad20", n) for n in range(12)] + [("ad21", n) for n in range(12)]
          + [("uv1", n) for n in range(128)]
          + [("min", n) for n in range(16)] + [("mout", n) for n in range(4)]
          + [("gin", n) for n in range(16)] + [("gab", 0)] + [("gout", n) for n in range(4)])


class Engine:

    def __init__(self, eng, sem):
        self.eng, self.sem, self.count, self.seen = eng, sem, 0, {}

    def wait(self, *tokens):
        for t in tokens:
            if t is None:
                continue
            sem, value = t
            if self.seen.get(sem.name, 0) < value:
                self.seen[sem.name] = value
                self.eng.wait_ge(sem, value)

    def __call__(self, make, *tokens):
        self.wait(*tokens)
        make().then_inc(self.sem, 1)
        self.count += 1
        return (self.sem, self.count)

    def quiet(self, make, *tokens):
        self.wait(*tokens)
        make()

    def now(self):
        return (self.sem, self.count)


class Slots:

    def __init__(self, items):
        self.items, self.free, self.n = list(items), {}, 0

    def take(self):
        i = self.n % len(self.items)
        self.n += 1
        return i, self.items[i], self.free.get(i, ())

    def done(self, i, *tokens):
        self.free[i] = tokens


def build(nc, w, cst_d, prm_d, rows_d, x_d, xT_d, cT_d, sguw_d, lng_d, out_d, upto=99, dbg=None):
    tns, vec, act, gps, syn = nc.tensor, nc.vector, nc.scalar, nc.gpsimd, nc.sync
    nsem = [0]

    def sem(name):
        nsem[0] += 1
        return nc.alloc_semaphore(name)

    T, V, A, G = Engine(tns, sem("pe")), Engine(vec, sem("dve")), Engine(act, sem("act")), Engine(gps, sem("pool"))
    S = Engine(syn, sem("sp"))

    def sb(name, n):
        return nc.alloc_sbuf_tensor(name, [128, n], F)

    ring = sb("ring", RING * 2048)
    XS = sb("XS", 2048)
    HT = sb("HT", 2048)
    TMP = sb("TMP", 2048)
    GR = sb("GR", 1024)
    LN = sb("LN", 2048)
    CP = sb("CP", CONST_AT["persist_end"][0])
    PR = sb("PR", PRM_N)
    RW = sb("RW", ROW_N)
    MOD = sb("MOD", 96 + 48 + 48)
    SIL = sb("SIL", 24)
    SM = sb("SM", 64)
    ARENA_N = 29000
    ARENA = sb("ARENA", ARENA_N)
    PS = nc.alloc_psum_tensor("PS", [128, 8, 512], F)

    xs = XS[:, :].rearrange("p (t d) -> p t d", t=2)
    tmp = TMP[:, :].rearrange("p (t d) -> p t d", t=2)
    hT = HT[:, :].rearrange("p (c t) -> p c t", c=8)
    lng, lnb = LN[:, 0:1024], LN[:, 1024:2048]

    def cp(name):
        a, n = CONST_AT[name]
        return CP[:, a:a + n]

    ident, ones, iota, iota16 = cp("ident"), cp("ones"), cp("iota"), cp("iota16")

    def prm(name):
        a, n = PRM_AT[name]
        return PR[:, a:a + n]

    def row(name):
        a, n = ROW_AT[name]
        return RW[:, a:a + n]

    class Arena:
        def __init__(self):
            self.at = 0

        def get(self, size, dims=None, **k):
            ap = ARENA[:, self.at:self.at + size]
            self.at += size
            assert self.at <= ARENA_N, self.at
            return ap.rearrange(dims, **k) if dims else ap

    def fence():
        now = [e.now() for e in (T, V, A, G) if e.count]
        for e in (T, V, A, G):
            e.wait(*now)

    def fetch(dst, src, *tokens, name=None):
        s = sem(f"ld{nsem[0]}")
        G.wait(*tokens)
        gps.dma_start(dst, src).then_inc(s, 16)
        return (s, 16)

    wsem = [sem(f"w{i}") for i in range(RING)]
    loaded = [0]
    released = {}

    def issue():
        n = loaded[0]
        if n >= len(STREAM):
            return
        kind, i = STREAM[n]
        slot = n % RING
        if n >= RING:
            S.wait(*released[n - RING])
        src = w[kind][i]
        syn.dma_start(ring[:, slot * 2048:slot * 2048 + src.shape[1]], src).then_inc(wsem[slot], 16)
        loaded[0] += 1

    used = [0]

    def weight(kind, i):
        n = used[0]
        assert STREAM[n] == (kind, i), (STREAM[n], kind, i)
        used[0] += 1
        if n == 0:
            for _ in range(RING):
                issue()
        slot = n % RING
        return n, ring[:, slot * 2048:(slot + 1) * 2048], (wsem[slot], 16 * (n // RING + 1))

    def release(n, *tokens):
        released[n] = tokens
        if n + RING == loaded[0]:
            issue()

    def mm(out, lhsT, rhs, start, stop, *tokens, inc=False):
        f = lambda: tns.matmul(out, lhsT, rhs, start=start, stop=stop)
        return T(f, *tokens) if inc else T.quiet(f, *tokens)

    k_c = fetch(CP[:, :], cst_d[:, 0:CONST_AT["persist_end"][0]])
    k_p = fetch(PR[:, :], prm_d)
    k_r = fetch(RW[:, :], rows_d.partition_broadcast(128))
    k_x = fetch(xs, x_d.rearrange("(t p) d -> p t d", p=128))
    for e in (T, V, A, G):
        e.wait(k_c, k_p)
    V.wait(k_r)
    A.wait(k_r)

    sil = SIL[:, 0:16].rearrange("p (c v) -> p c v", v=2)
    sil2 = SIL[:, 16:24]
    A(lambda: act.activation(sil[:, :, 0], prm("c"), ACT.Silu))
    A(lambda: act.activation(sil[:, :, 1], prm("cc"), ACT.Silu))
    k_sil = A(lambda: act.activation(sil2, prm("c2"), ACT.Silu))

    mod0 = MOD[:, 0:96].rearrange("p (n v) -> p n v", v=2)
    mod1 = MOD[:, 96:144]
    mod2 = [MOD[:, 144:168], MOD[:, 168:192]]

    def ada(kind, items, nv, cs, bank, *tokens):
        tok = None
        T.wait(k_sil, *tokens)
        for n in range(items):
            i, slot, k = weight(kind, n)
            wt = slot.rearrange("p (c f) -> p c f", c=8)
            for b in range(2):
                o = PS[:, bank, (2 * n + b) * nv:(2 * n + b + 1) * nv]
                for c in range(8):
                    tok = mm(o, wt[:, c, b * 128:(b + 1) * 128], cs[:, c * nv:(c + 1) * nv],
                             c == 0, c == 7, k, inc=(c == 7 and b == 1))
            release(i, tok)
        return tok

    k_ada = ada("ada0", 24, 2, SIL[:, 0:16], 0)
    k = V(lambda: vec.tensor_tensor(mod0, PS[:, 0, 0:96].rearrange("p (n v) -> p n v", v=2),
                                    prm("ab0").unsqueeze(2).to_broadcast([128, 48, 2]), ALU.add), k_ada)
    k = V(lambda: vec.tensor_scalar(mod0[:, 8:16, :], mod0[:, 8:16, :], 1.0, None, ALU.add), k)
    k_mod0 = V(lambda: vec.tensor_scalar(mod0[:, 32:40, :], mod0[:, 32:40, :], 1.0, None, ALU.add), k)

    def gate_rows(cols, banks, k_cols, k_free=()):
        d = TMP[:, 0:1024].rearrange("p (c m) -> p c m", c=8)
        k1 = V(lambda: vec.tensor_tensor(d, ident.unsqueeze(1).to_broadcast([128, 8, 128]),
                                         cols.unsqueeze(2).to_broadcast([128, 8, 128]), ALU.mult),
               k_cols, *k_free)
        for b in range(2):
            k2 = mm(PS[:, banks[b], :], ones, TMP[:, b * 512:(b + 1) * 512], True, True, k1, inc=True)
        for b in range(2):
            k3 = A(lambda: act.copy(GR[:, b * 512:(b + 1) * 512], PS[:, banks[b], :]), k2)
        return k3

    def modulated(dst, sc, sh, src, *tokens):
        for c in range(8):
            s1, s2 = sc[:, c:c + 1], sh[:, c:c + 1]
            t = V(lambda: vec.tensor_scalar(dst[:, c, :], src[:, c, :], s1, s2, ALU.mult, ALU.add), *tokens)
        return t

    def make_hT(sc, sh, banks):
        fence()
        t = None
        for q in range(4):
            b = banks[q % len(banks)]
            for j in range(4):
                c, tb = 2 * q + j // 2, j % 2
                f = lambda: tns.transpose(PS[:, b, j * 128:(j + 1) * 128], xs[:, tb, c * 128:(c + 1) * 128], ident)
                kt = T(f) if j == 3 else T.quiet(f)
            for jj in range(2):
                c = 2 * q + jj
                if q % 2 == 0:
                    t = V(lambda: vec.tensor_scalar(hT[:, c, :], PS[:, b, jj * 256:jj * 256 + 256], sc[:, c:c + 1], sh[:, c:c + 1],
                                                    ALU.mult, ALU.add), kt)
                else:
                    u = A(lambda: act.activation(hT[:, c, :], PS[:, b, jj * 256:jj * 256 + 256], ACT.Identity,
                                                 bias=sh[:, c:c + 1], scale=sc[:, c:c + 1]), kt)
        fence()

    def residual_ln(ln_i, k_ln, banks, k_y):
        st = SM[:, 0:24]
        mv = SM[:, 24:28]
        rs = SM[:, 28:30]
        k2 = []
        for tb in range(2):
            for nh in range(2):
                sl = slice(nh * 512, nh * 512 + 512)
                k1 = V(lambda: vec.tensor_tensor(tmp[:, tb, sl], PS[:, banks[tb][nh], :], GR[:, sl], ALU.mult), *k_y)
                k1 = V(lambda: vec.scalar_tensor_tensor(xs[:, tb, sl], xs[:, tb, sl], ALPHA, tmp[:, tb, sl],
                                                        ALU.mult, ALU.add), k1)
                o = (tb * 2 + nh) * 6
                k1 = V(lambda: vec.bn_stats(st[:, o:o + 6], xs[:, tb, sl]), k1)
            k2.append(V(lambda: vec.bn_aggr(mv[:, 2 * tb:2 * tb + 2], st[:, tb * 12:tb * 12 + 12]), k1))
        m2 = mv.rearrange("p (t s) -> p t s", s=2)
        k3 = V(lambda: vec.tensor_scalar(rs, m2[:, :, 1], 1e-5, None, ALU.add), *k2)
        k3 = A(lambda: act.sqrt(rs, rs), k3)
        k3 = V(lambda: vec.reciprocal(rs, rs), k3)
        V.wait(*k_ln)
        for tb in range(2):
            k4 = V(lambda: vec.tensor_scalar(xs[:, tb, :], xs[:, tb, :], mv[:, 2 * tb:2 * tb + 1], rs[:, tb:tb + 1],
                                             ALU.subtract, ALU.mult), k3)
            k4 = V(lambda: vec.tensor_tensor(xs[:, tb, :], xs[:, tb, :], lng, ALU.mult), k4)
            k4 = V(lambda: vec.tensor_tensor(xs[:, tb, :], xs[:, tb, :], lnb, ALU.add), k4)
        return k4

    def load_ln(i):
        s = [fetch(LN[:, 1024 * j:1024 * j + 1024], lng_d[2 * i + j:2 * i + j + 1, :].rearrange("a d -> (a d)")
                   .partition_broadcast(128), V.now()) for j in range(2)]
        return s

    def rows_out(kind, lhs, nk, banks, k_in):
        t = None
        T.wait(*k_in)
        n = 0
        for nh in range(2):
            for kg in range(nk // 4):
                i, slot, k = weight(kind, n)
                n += 1
                wt = slot.rearrange("p (c f) -> p c f", c=4)
                for tb in range(2):
                    for c in range(4):
                        kc = kg * 4 + c
                        t = mm(PS[:, banks[tb][nh], :], lhs[:, kc, tb * 128:(tb + 1) * 128], wt[:, c, :],
                               kc == 0, kc == nk - 1, k, inc=(c == 3))
                release(i, t)
        return t

    ar = Arena()
    qT = ar.get(2048, "p (h t) -> p h t", h=8)
    kT = ar.get(4096, "p (h t) -> p h t", h=8)
    va = ar.get(4096, "p (b e) -> p b e", b=4)
    gg = ar.get(2048, "p (t e) -> p t e", t=2)
    hcT = ar.get(2048, "p (c t) -> p c t", c=8)
    catT = ar.get(3072, "p (c t) -> p c t", c=12)
    rope = ar.get(640)
    sguw = ar.get(512, "p (g q) -> p g q", g=4)
    k_rope = fetch(rope, cst_d[:, CONST_AT["cos"][0]:CONST_AT["rope_end"][0]])
    k_sgw = fetch(sguw, sguw_d)
    cosT, sinT, perm = rope[:, 0:256], rope[:, 256:512], rope[:, 512:640]
    k_xT = fetch(hT, xT_d.rearrange("(c p) t -> p c t", p=128))
    k_cT = fetch(hcT, cT_d.rearrange("(c p) t -> p c t", p=128))
    k_ln = load_ln(0)
    modulated(hT, mod0[:, 8:16, 0], mod0[:, 0:8, 0], hT, k_mod0, k_xT)
    k_h = modulated(hcT, mod0[:, 8:16, 1], mod0[:, 0:8, 1], hcT, k_mod0, k_cT)

    raws = Slots([ar.get(256) for _ in range(2)])
    tms = Slots([ar.get(256) for _ in range(2)])
    pb = Slots(range(8))
    T.wait(k_h)
    V.wait(k_rope)
    T.wait(k_rope)

    def projT(wt, b, rhs, out, k):
        for c in range(8):
            t = mm(out, wt[:, c, b * 128:(b + 1) * 128], rhs[:, c, :], c == 0, c == 7, k, inc=(c == 7))
        return t

    def projR(wt, lhs, tb, out, k):
        for c in range(8):
            t = mm(out, lhs[:, c, tb * 128:(tb + 1) * 128], wt[:, c, :], c == 0, c == 7, k, inc=(c == 7))
        return t

    for n in range(8):
        i, slot, k = weight("abin", n)
        wt = slot.rearrange("p (c f) -> p c f", c=8)
        for b in range(2):
            h = (2 * n + b) % 8
            dst = qT[:, h, :] if n < 4 else kT[:, h, 256:512]
            if n >= 4:
                bi, bk, fr = pb.take()
                T.wait(*fr)
                t = projT(wt, b, hcT, PS[:, bk, 0:256], k)
                pb.done(bi, A(lambda: act.copy(kT[:, h, 0:256], PS[:, bk, 0:256]), t))
            bi, bk, fr = pb.take()
            T.wait(*fr)
            t = projT(wt, b, hT, PS[:, bk, 0:256], k)
            if b == 1:
                release(i, t)
            ri, raw, rf = raws.take()
            k1 = A(lambda: act.copy(raw, PS[:, bk, 0:256]), t, *rf)
            t2 = mm(PS[:, bk, 256:512], perm, raw, True, True, k1, inc=True)
            raws.done(ri, t2)
            mi, tm, mf = tms.take()
            k2 = V(lambda: vec.tensor_tensor(tm, PS[:, bk, 0:256], cosT, ALU.mult), t2, *mf)
            k3 = V(lambda: vec.tensor_tensor(dst, PS[:, bk, 256:512], sinT, ALU.mult), t2)
            pb.done(bi, k3)
            k4 = V(lambda: vec.tensor_tensor(dst, dst, tm, ALU.add), k2, k3)
            tms.done(mi, k4)
    for n in range(8, 16):
        i, slot, k = weight("abin", n)
        wt = slot.rearrange("p (c f) -> p c f", c=8)
        if n < 12:
            blocks = [(hcT, 0, va[:, 0, :]), (hcT, 1, va[:, 1, :]), (hT, 0, va[:, 2, :]), (hT, 1, va[:, 3, :])]
            at = (n - 8) * 256
        else:
            blocks = [(hT, 0, gg[:, 0, :]), (hT, 1, gg[:, 1, :])]
            at = (n - 12) * 256
        for src, tb, dst in blocks:
            bi, bk, fr = pb.take()
            T.wait(*fr)
            t = projR(wt, src, tb, PS[:, bk, 0:256], k)
            if n < 12:
                e = A(lambda: act.copy(dst[:, at:at + 256], PS[:, bk, 0:256]), t)
            else:
                e = A(lambda: act.activation(dst[:, at:at + 256], PS[:, bk, 0:256], ACT.Gelu_apprx_tanh), t)
            pb.done(bi, e)
        release(i, t)
    fence()

    lam = SM[:, 32:36]
    lr = row("lam").rearrange("p (a b d) -> p a b d", a=2, b=2)
    k1 = V(lambda: vec.tensor_tensor(TMP[:, 0:128].rearrange("p (a d) -> p a d", a=2), lr[:, :, 0, :], lr[:, :, 1, :],
                                     ALU.mult))
    k1 = V(lambda: vec.tensor_reduce(lam[:, 0:2], TMP[:, 0:128].rearrange("p (a d) -> p a d", a=2), AX, ALU.add), k1)
    k1 = A(lambda: act.activation(lam[:, 0:2], lam[:, 0:2], ACT.Exp), k1)
    k1 = V(lambda: vec.tensor_tensor(lam[:, 2:3], lam[:, 0:1], lam[:, 1:2], ALU.subtract), k1)
    lam_init = 0.8 - 0.6 * math.exp(-0.3 * 0)
    k_lam = V(lambda: vec.tensor_scalar(lam[:, 3:4], lam[:, 2:3], lam_init, -1.0, ALU.add, ALU.mult), k1)

    gu, gv = gg[:, :, 0:512], gg[:, :, 512:1024]
    st = SM[:, 0:12]
    mv = SM[:, 24:28]
    m2 = mv.rearrange("p (t s) -> p t s", s=2)
    rs = SM[:, 28:30]
    for tb in range(2):
        k1 = V(lambda: vec.bn_stats(st[:, tb * 6:tb * 6 + 6], gv[:, tb, :]))
        k1 = V(lambda: vec.bn_aggr(mv[:, 2 * tb:2 * tb + 2], st[:, tb * 6:tb * 6 + 6]), k1)
    k1 = V(lambda: vec.tensor_scalar(rs, m2[:, :, 1], 1e-5, None, ALU.add), k1)
    k1 = A(lambda: act.sqrt(rs, rs), k1)
    k1 = V(lambda: vec.reciprocal(rs, rs), k1)
    for tb in range(2):
        k2 = V(lambda: vec.tensor_scalar(gv[:, tb, :], gv[:, tb, :], mv[:, 2 * tb:2 * tb + 1], rs[:, tb:tb + 1],
                                         ALU.subtract, ALU.mult), k1)
        k2 = V(lambda: vec.tensor_tensor(gv[:, tb, :], gv[:, tb, :], row("sg"), ALU.mult), k2)
        k2 = V(lambda: vec.tensor_tensor(gv[:, tb, :], gv[:, tb, :], row("sb"), ALU.add), k2)
        T.wait(k_sgw)
        for g in range(4):
            t = mm(PS[:, tb, g * 128:(g + 1) * 128], sguw[:, g, :], gv[:, tb, g * 128:(g + 1) * 128], True, True,
                   k2, inc=(g == 3))
        for g in range(4):
            sl = slice(g * 128, (g + 1) * 128)
            k3 = V(lambda: vec.scalar_tensor_tensor(gu[:, tb, sl], PS[:, tb, sl], prm("sgub")[:, g:g + 1],
                                                    gu[:, tb, sl], ALU.add, ALU.mult), t)
        for g in range(4):
            f = lambda: tns.transpose(PS[:, 2 + tb, g * 128:(g + 1) * 128], gu[:, tb, g * 128:(g + 1) * 128], ident)
            t = T(f, k3) if g == 3 else T.quiet(f, k3)
        A(lambda: act.copy(catT[:, 8:12, tb * 128:(tb + 1) * 128],
                           PS[:, 2 + tb, :].rearrange("p (g q) -> p g q", g=4)), t)
    fence()

    O = ar.get(2048, "p (t e) -> p t e", t=2)
    pP = Slots([ar.get(1024, "p (m k) -> p m k", m=2) for _ in range(3)])
    pA = Slots([ar.get(512) for _ in range(2)])
    pT = Slots([ar.get(512) for _ in range(2)])
    sB = Slots([0, 1, 2, 3])
    tB = Slots([4, 5])
    oB = Slots([6, 7])
    stt = Slots([SM[:, 36 + 8 * i:44 + 8 * i] for i in range(3)])
    units = [(h, qb) for h in range(8) for qb in range(2)]
    live = {}

    def scores(u):
        h, qb = units[u]
        pi, P, pf = pP.take()
        si, s8, sf = stt.take()
        ks = []
        for m in range(2):
            bi, bk, fr = sB.take()
            t = mm(PS[:, bk, :], qT[64 * m:64 * m + 64, h, qb * 128:(qb + 1) * 128], kT[64 * m:64 * m + 64, h, :],
                   True, True, *fr, inc=True)
            k1 = V(lambda: vec.tensor_reduce(s8[:, m:m + 1], PS[:, bk, :], AX, ALU.max), t, *sf)
            k1 = V(lambda: vec.tensor_scalar(s8[:, 2 + m:3 + m], s8[:, m:m + 1], -0.125, None, ALU.mult), k1)
            k1 = A(lambda: act.activation(P[:, m, :], PS[:, bk, :], ACT.Exp, bias=s8[:, 2 + m:3 + m], scale=0.125,
                                          accum_out=s8[:, 4 + m:5 + m]), k1, *pf)
            sB.done(bi, k1)
            ks.append(k1)
        live[u] = (pi, P, si, s8, ks)

    def combine(u):
        pi, P, si, s8, ks = live[u]
        ai, Am, af = pA.take()
        k1 = V(lambda: vec.reciprocal(s8[:, 6:8], s8[:, 4:6]), *ks)
        k2 = V(lambda: vec.tensor_tensor(s8[:, 7:8], s8[:, 7:8], lam[:, 3:4], ALU.mult), k1, k_lam)
        k3 = V(lambda: vec.tensor_scalar(P[:, 1, :], P[:, 1, :], s8[:, 7:8], None, ALU.mult), k2)
        k4 = V(lambda: vec.scalar_tensor_tensor(Am, P[:, 0, :], s8[:, 6:7], P[:, 1, :], ALU.mult, ALU.add), k3, *af)
        pP.done(pi, k4)
        stt.done(si, k4)
        live[u] = (ai, Am, k4)

    def turn(u):
        ai, Am, k4 = live[u]
        bi, bk, fr = tB.take()
        ti, At, tf = pT.take()
        T.wait(k4, *fr)
        for j in range(4):
            f = lambda: tns.transpose(PS[:, bk, j * 128:(j + 1) * 128], Am[:, j * 128:(j + 1) * 128], ident)
            t = T(f) if j == 3 else T.quiet(f)
        pA.done(ai, t)
        k5 = A(lambda: act.copy(At, PS[:, bk, :]), t, *tf)
        tB.done(bi, k5)
        live[u] = (ti, At, k5)

    def values(u):
        h, qb = units[u]
        ti, At, k5 = live[u]
        bi, bk, fr = oB.take()
        T.wait(k5, *fr)
        for j in range(4):
            t = mm(PS[:, bk, 0:128], At[:, j * 128:(j + 1) * 128], va[:, j, h * 128:(h + 1) * 128], j == 0, j == 3,
                   inc=(j == 3))
        pT.done(ti, t)
        oB.done(bi, V(lambda: vec.tensor_copy(O[:, qb, h * 128:(h + 1) * 128], PS[:, bk, 0:128]), t))

    for s in range(len(units) + 3):
        for stage, lag in ((scores, 0), (combine, 1), (turn, 2), (values, 3)):
            if 0 <= s - lag < len(units):
                stage(s - lag)
    fence()

    def head_norm(O, gain, scale, eps, k=None):
        o3 = O.rearrange("p t (h e) -> p (t h) e", e=128)
        t3 = TMP[:, :].rearrange("p (n e) -> p n e", e=128)
        r = SM[:, 0:16]
        k1 = V(lambda: vec.tensor_tensor(t3, o3, o3, ALU.mult), k)
        k1 = V(lambda: vec.tensor_reduce(r, t3, AX, ALU.add), k1)
        k1 = V(lambda: vec.tensor_scalar(r, r, 1.0 / 128, eps, ALU.mult, ALU.add), k1)
        k1 = A(lambda: act.sqrt(r, r), k1)
        k1 = V(lambda: vec.reciprocal(r, r), k1)
        k1 = V(lambda: vec.tensor_tensor(t3, o3, r.unsqueeze(2).to_broadcast([128, 16, 128]), ALU.mult), k1)
        g3 = gain.unsqueeze(1).to_broadcast([128, 16, 128])
        k1 = V(lambda: vec.tensor_tensor(o3, t3, g3, ALU.mult), k1)
        if scale != 1.0:
            k1 = V(lambda: vec.tensor_scalar(o3, o3, scale, None, ALU.mult), k1)
        return k1

    k1 = head_norm(O, row("dng"), 1.0 - lam_init, 1e-5)

    def rows_to_T(src, dst, n, banks, k):
        b4 = Slots(banks)
        for q in range(n // 2):
            bi, bk, fr = b4.take()
            T.wait(k, *fr)
            for j in range(4):
                c, tb = 2 * q + j // 2, j % 2
                f = lambda: tns.transpose(PS[:, bk, j * 128:(j + 1) * 128], src[:, tb, c * 128:(c + 1) * 128], ident)
                t = T(f) if j == 3 else T.quiet(f)
            o = dst[:, 2 * q:2 * q + 2, :].rearrange("p c t -> p (c t)")
            e = A(lambda: act.copy(o, PS[:, bk, :]), t)
            b4.done(bi, e)
        return e

    k1 = rows_to_T(O, catT[:, 0:8, :], 8, [4, 5, 6, 7], k1)
    kg = gate_rows(mod0[:, 16:24, 0], [6, 7], k_mod0, (k1,))
    YB = [[0, 1], [2, 3]]
    k_y = rows_out("about", catT, 12, YB, (k1,))
    V.wait(k_x)
    residual_ln(0, k_ln, YB, (k_y, kg))

    if dbg is not None and upto == 0:
        s = sem("dbg")
        S.wait(V.now())
        syn.dma_start(dbg.rearrange("(t p) d -> p t d", p=128), xs).then_inc(s, 16)
        syn.wait_ge(s, 16)
        return

    def peer(layer, sc, sh, gate_cols, k_gc, between):
        make_hT(sc, sh, [0, 1, 2, 3])
        ar = Arena()
        W = ar.get(128 * 2 * PW, "p (j t) -> p j t", j=PW)
        i1T, i2T, gT = ar.get(256), ar.get(256), ar.get(256)
        As = Slots([ar.get(128) for _ in range(4)])
        Bs = Slots([ar.get(PW) for _ in range(4)])
        Gs = Slots([ar.get(256) for _ in range(3)])
        Cs = Slots([ar.get(256) for _ in range(3)])
        TS = ar.get(512)
        TI = ar.get(512)
        TIf = ar.get(512)
        BS = ar.get(256)
        BP = ar.get(256)
        E = ar.get(256)
        pi, pj = ar.get(256), ar.get(256)
        x1, x2 = ar.get(256), ar.get(256)
        rr = ar.get(16)
        tp = Arena()
        qT = tp.get(4096, "p (h t) -> p h t", h=16)
        sc_, sc2 = tp.get(4096, "p (t n) -> p t n", t=2), tp.get(4096, "p (t n) -> p t n", t=2)
        big = tp.get(2048)
        pb = Slots(range(8))
        for n in range(8):
            i, slot, k = weight(f"wq{layer}", n)
            wt = slot.rearrange("p (c f) -> p c f", c=8)
            for b in range(2):
                bi, bk, fr = pb.take()
                T.wait(*fr)
                t = projT(wt, b, hT, PS[:, bk, 0:256], k)
                k_q = A(lambda: act.copy(qT[:, 2 * n + b, :], PS[:, bk, 0:256]), t)
                pb.done(bi, k_q)
            release(i, t)
        i, slot, k = weight(f"keys{layer}", 0)
        kys = slot.rearrange("p (h n) -> p h n", h=16)
        T.wait(k_q)
        k_s = []
        for tb in range(2):
            for q in range(4):
                bi, bk, fr = pb.take()
                T.wait(*fr)
                for j in range(4):
                    hp = 4 * q + j
                    t = mm(PS[:, bk, j * 128:(j + 1) * 128], qT[:, hp, tb * 128:(tb + 1) * 128], kys[:, hp, :],
                           True, True, k, inc=(j == 3))
                e = A(lambda: act.copy(sc_[:, tb, q * 512:(q + 1) * 512], PS[:, bk, :]), t)
                pb.done(bi, e)
                k_s.append(e)
        release(i, t)
        T.wait(*k_s)
        k_btw = between(T)
        TIu, BPu, pju, piu = TI.bitcast(U32), BP.bitcast(U32), pj.bitcast(U32), pi.bitcast(U32)
        BIG = -3.0e38

        def top16(vals, idx, src, work, n, width, ready):
            a, b, c, d = {}, {}, {}, {}
            for r in range(n):
                s = src[:, r * width:(r + 1) * width]
                a[r] = V(lambda: vec.max(vals[:, 16 * r:16 * r + 8], s), ready[r])
            for r in range(n):
                s, z = src[:, r * width:(r + 1) * width], work[:, r * width:(r + 1) * width]
                b[r] = V(lambda: vec.match_replace(z, vals[:, 16 * r:16 * r + 8], s, BIG), a[r])
                V(lambda: vec.max_index(idx[:, 16 * r:16 * r + 8], vals[:, 16 * r:16 * r + 8], s))
            for r in range(n):
                z = work[:, r * width:(r + 1) * width]
                c[r] = V(lambda: vec.max(vals[:, 16 * r + 8:16 * r + 16], z), b[r])
            for r in range(n):
                z = work[:, r * width:(r + 1) * width]
                d[r] = V(lambda: vec.max_index(idx[:, 16 * r + 8:16 * r + 16], vals[:, 16 * r + 8:16 * r + 16], z), c[r])
            return d[n - 1]

        for tb in range(2):
            o = tb * 256
            kk = top16(TS[:, o:o + 256], TIu[:, o:o + 256], sc_[:, tb, :], sc2[:, tb, :], 16, 128,
                       {r: k_s[4 * tb + r // 4] for r in range(16)})
            t4 = TS[:, o:o + 256].rearrange("p (h s k) -> p h s k", s=2, k=16)
            cand = sc_[:, tb, :].rearrange("p (h a b) -> p h a b", h=8, a=16)
            kk = V(lambda: vec.tensor_tensor(cand, t4[:, :, 0, :].unsqueeze(3).to_broadcast([128, 8, 16, 16]),
                                             t4[:, :, 1, :].unsqueeze(2).to_broadcast([128, 8, 16, 16]), ALU.add), kk)
            b = tb * 128
            kk = top16(BS[:, b:b + 128], BPu[:, b:b + 128], sc_[:, tb, :], sc2[:, tb, :], 8, 256,
                       {r: kk for r in range(8)})
        b3 = BS.rearrange("p (n k) -> p n k", k=16)
        e3 = E.rearrange("p (n k) -> p n k", k=16)
        k1 = V(lambda: vec.tensor_tensor(e3, b3, b3[:, :, 0:1].to_broadcast([128, 16, 16]), ALU.subtract), kk)
        k_e = A(lambda: act.activation(E, E, ACT.Exp), k1)
        k2 = V(lambda: vec.tensor_scalar(piu, BPu, 4, None, ALU.logical_shift_right), kk)
        k3 = V(lambda: vec.tensor_scalar(pju, BPu, 15, None, ALU.bitwise_and), kk)
        k4 = V(lambda: vec.tensor_copy(TIf, TIu), kk)
        k2 = V(lambda: vec.tensor_copy(x1, piu), k2)
        k3 = V(lambda: vec.tensor_copy(x2, pju), k3)
        k2 = V(lambda: vec.tensor_copy(pi, x1), k2)
        k3 = V(lambda: vec.tensor_copy(pj, x2), k3)
        bg = big.rearrange("p (n a) -> p n a", a=16)
        bg4 = big.rearrange("p (h k a) -> p h k a", h=8, k=16)
        last = None
        for tb in range(2):
            for s, (pos, dst) in enumerate(((pi, x1), (pj, x2))):
                tt = TIf[:, tb * 256:(tb + 1) * 256].rearrange("p (h s a) -> p h s a", s=2, a=16)[:, :, s, :]
                ps = pos[:, tb * 128:(tb + 1) * 128]
                k5 = V(lambda: vec.tensor_tensor(bg, iota16.unsqueeze(1).to_broadcast([128, 128, 16]),
                                                 ps.unsqueeze(2).to_broadcast([128, 128, 16]), ALU.is_equal),
                       k2, k3, k4, last)
                k5 = V(lambda: vec.tensor_tensor(bg4, bg4, tt.unsqueeze(2).to_broadcast([128, 8, 16, 16]), ALU.mult),
                       k5)
                last = V(lambda: vec.tensor_reduce(dst[:, tb * 128:(tb + 1) * 128], bg, AX, ALU.add), k5)
        k6 = V(lambda: vec.tensor_reduce(rr, e3, AX, ALU.add), k_e)
        k6 = V(lambda: vec.reciprocal(rr, rr), k6)
        k6 = V(lambda: vec.tensor_tensor(e3, e3, rr.unsqueeze(2).to_broadcast([128, 16, 16]), ALU.mult), k6)
        k7 = None
        for n, (src, dst) in enumerate(((x1, i1T), (x2, i2T), (E, gT))):
            for tb in range(2):
                t = T(lambda: tns.transpose(PS[:, n, tb * 128:(tb + 1) * 128], src[:, tb * 128:(tb + 1) * 128], ident),
                      last, k6)
            k7 = A(lambda: act.copy(dst, PS[:, n, 0:256]), t)
        fence()
        kg = gate_rows(gate_cols, [6, 7], k_gc)
        k_ln = load_ln(2 * layer + 1)
        fence()

        wb = Slots([6, 7])
        ub = Slots([4, 5])
        per = 512 // PW
        k_w = None
        first, final = True, None
        for part in range(NPART):
            if part:
                fence()
            for g in range(256 // per):
                bi, bk, fr = wb.take()
                T.wait(*fr)
                for r in range(per):
                    tok = g * per + r
                    ai, Am, af = As.take()
                    ci, Bm, bf = Bs.take()
                    k1 = V(lambda: vec.tensor_scalar(Am, iota, i1T[:, tok:tok + 1], None, ALU.is_equal), *af)
                    k2 = V(lambda: vec.tensor_scalar(Bm, iota[:, part * PW:(part + 1) * PW], i2T[:, tok:tok + 1],
                                                     gT[:, tok:tok + 1], ALU.is_equal, ALU.mult), *bf)
                    t = mm(PS[:, bk, r * PW:(r + 1) * PW], Am, Bm, True, True, k2, inc=True)
                    As.done(ai, t)
                    Bs.done(ci, t)
                k_w = A(lambda: act.copy(W[:, :, g * per:(g + 1) * per],
                                         PS[:, bk, :].rearrange("p (t j) -> p j t", j=PW)), t)
                wb.done(bi, k_w)
            held = {}

            def up(j):
                n = part * PW + j
                i, slot, k = weight(f"uv{layer}", n)
                ut = slot[:, 0:1024].rearrange("p (c e) -> p c e", c=8)
                bi, bk, fr = ub.take()
                T.wait(*fr)
                for c in range(8):
                    t = mm(PS[:, bk, 0:256], ut[:, c, :], hT[:, c, :], c == 0, c == 7, k, inc=(c == 7))
                gi, Gt, gf = Gs.take()
                k1 = A(lambda: act.activation(Gt, PS[:, bk, 0:256], ACT.Gelu_apprx_tanh), t, *gf)
                ub.done(bi, k1)
                ci, Ct, cf = Cs.take()
                k2 = V(lambda: vec.tensor_tensor(Ct, Gt, W[:, j, :], ALU.mult), k1, k_w, *cf)
                Gs.done(gi, k2)
                held[j] = (i, slot, ci, Ct, k2)

            def down(j):
                i, slot, ci, Ct, k2 = held.pop(j)
                T.wait(k2)
                for tb in range(2):
                    for nh in range(2):
                        t = mm(PS[:, YB[tb][nh], :], Ct[:, tb * 128:(tb + 1) * 128],
                               slot[:, 1024 + nh * 512:1536 + nh * 512], part == 0 and j == 0,
                               part == NPART - 1 and j == PW - 1, inc=(tb == 1 and nh == 1))
                Cs.done(ci, t)
                release(i, t)
                return t

            for j in range(PW + 1):
                if j < PW:
                    up(j)
                if j >= 1:
                    k_y = down(j - 1)
        residual_ln(2 * layer + 1, k_ln, YB, (k_y, kg))

    def btw0(T):
        t = ada("ada1", 24, 1, sil1, 0, )
        k = V(lambda: vec.tensor_tensor(mod1, PS[:, 0, 0:48], prm("ab1"), ALU.add), t)
        for a in (8, 32):
            k = V(lambda: vec.tensor_scalar(mod1[:, a:a + 8], mod1[:, a:a + 8], 1.0, None, ALU.add), k)
        return k

    def btw1(T):
        k = None
        for l in range(2):
            t = ada(f"ad2{l}", 12, 1, sil2, l)
            k = V(lambda: vec.tensor_tensor(mod2[l], PS[:, l, 0:24], prm(f"a2{l}"), ALU.add), t)
            k = V(lambda: vec.tensor_scalar(mod2[l][:, 8:16], mod2[l][:, 8:16], 1.0, None, ALU.add), k)
        return k

    sil1 = SM[:, 54:62]
    V(lambda: vec.tensor_copy(sil1, sil[:, :, 0]))
    fence()
    peer(0, mod0[:, 32:40, 0], mod0[:, 24:32, 0], mod0[:, 40:48, 0], None, btw0)

    def dump():
        s = sem("dbg")
        S.wait(V.now())
        syn.dma_start(dbg.rearrange("(t p) d -> p t d", p=128), xs).then_inc(s, 16)
        syn.wait_ge(s, 16)

    if dbg is not None and upto == 1:
        return dump()

    make_hT(mod1[:, 8:16], mod1[:, 0:8], [0, 1, 2, 3])
    k_ln = load_ln(2)
    ar = Arena()
    z = ar.get(2048, "p (t e) -> p t e", t=2)
    pm = ar.get(2048, "p (b g t) -> p b g t", b=2, g=4)
    mT = ar.get(2048, "p (c t) -> p c t", c=8)
    eT = ar.get(2048, "p (c t) -> p c t", c=8)
    k_pm = fetch(pm.rearrange("p b g t -> p (b g t)"), cst_d[:, CONST_AT["pool"][0]:CONST_AT["pool"][0] + 2048],
                 T.now(), V.now(), A.now())
    pb = Slots(range(8))
    for n in range(4):
        i, slot, k = weight("pin", n)
        wt = slot.rearrange("p (c f) -> p c f", c=8)
        for tb in range(2):
            bi, bk, fr = pb.take()
            T.wait(*fr)
            t = projR(wt, hT, tb, PS[:, bk, 0:256], k)
            k1 = A(lambda: act.copy(z[:, tb, n * 256:(n + 1) * 256], PS[:, bk, 0:256]), t)
            pb.done(bi, k1)
        release(i, t)
    T.wait(k1, k_pm)
    for c in range(8):
        bi, bk, fr = pb.take()
        T.wait(*fr)
        for b in range(2):
            t = mm(PS[:, bk, 0:256], z[:, b, c * 128:(c + 1) * 128], pm[:, b, c // 2, :], b == 0, b == 1, inc=(b == 1))
        k1 = A(lambda: act.copy(mT[:, c, :], PS[:, bk, 0:256]), t)
        pb.done(bi, k1)
    i, slot, k = weight("pgrp", 0)
    wt = slot.rearrange("p (g c e) -> p g c e", g=4, c=2)
    T.wait(k1)
    for c in range(8):
        bi, bk, fr = pb.take()
        T.wait(*fr)
        for b in range(2):
            t = mm(PS[:, bk, 0:256], wt[:, c // 2, b, (c % 2) * 128:(c % 2 + 1) * 128], mT[:, 2 * (c // 2) + b, :],
                   b == 0, b == 1, k, inc=(b == 1))
        k1 = A(lambda: act.activation(eT[:, c, :], PS[:, bk, 0:256], ACT.Copy, scale=prm("psc")[:, c:c + 1]), t)
        pb.done(bi, k1)
    release(i, t)
    kg = gate_rows(mod1[:, 16:24], [6, 7], None, (k1,))
    T.wait(kg)
    k_y = rows_out("pout", eT, 8, YB, (k1,))
    residual_ln(2, k_ln, YB, (k_y, kg))
    if dbg is not None and upto == 2:
        return dump()
    peer(1, mod1[:, 32:40], mod1[:, 24:32], mod1[:, 40:48], None, btw1)
    if dbg is not None and upto == 3:
        return dump()

    make_hT(mod2[0][:, 8:16], mod2[0][:, 0:8], [0, 1, 2, 3])
    k_ln = load_ln(4)
    ar = Arena()
    qT = ar.get(2048, "p (h t) -> p h t", h=8)
    kT = ar.get(2048, "p (h t) -> p h t", h=8)
    va = ar.get(2048, "p (b e) -> p b e", b=2)
    zT = ar.get(2048, "p (h t) -> p h t", h=8)
    oT = ar.get(2048, "p (h t) -> p h t", h=8)
    cm = ar.get(128)
    k_cm = fetch(cm, cst_d[:, CONST_AT["causal"][0]:CONST_AT["causal"][0] + 128], T.now(), V.now(), A.now())
    pb = Slots(range(8))
    for n in range(16):
        i, slot, k = weight("min", n)
        wt = slot.rearrange("p (c f) -> p c f", c=8)
        for b in range(2):
            bi, bk, fr = pb.take()
            T.wait(*fr)
            if 8 <= n < 12:
                t = projR(wt, hT, b, PS[:, bk, 0:256], k)
                e = A(lambda: act.copy(va[:, b, (n - 8) * 256:(n - 7) * 256], PS[:, bk, 0:256]), t)
            else:
                t = projT(wt, b, hT, PS[:, bk, 0:256], k)
                h = (2 * n + b) % 8
                if n < 8:
                    e = A(lambda: act.copy((qT if n < 4 else kT)[:, h, :], PS[:, bk, 0:256]), t)
                else:
                    e = A(lambda: act.activation(zT[:, h, :], PS[:, bk, 0:256], ACT.Silu), t)
            pb.done(bi, e)
        release(i, t)
    fence()
    V.wait(k_cm)
    SC2 = 128.0 ** -0.5
    sS = Slots([ar.get(256) for _ in range(3)])
    pT = Slots([ar.get(384) for _ in range(2)])
    sB, tB, oB = Slots([0, 1, 2]), Slots([3, 4, 5]), Slots([6, 7])
    stt = Slots([SM[:, 8 * i:8 * i + 4] for i in range(4)])
    units = [(h, qb) for h in range(8) for qb in range(2)]

    def scores2(u):
        h, qb = units[u]
        nk = 128 * (qb + 1)
        si, Sm, sf = sS.take()
        ti, s4, tf = stt.take()
        bi, bk, fr = sB.take()
        t = mm(PS[:, bk, 0:nk], qT[:, h, qb * 128:(qb + 1) * 128], kT[:, h, 0:nk], True, True, *fr, inc=True)
        k1 = V(lambda: vec.tensor_tensor(Sm[:, nk - 128:nk], PS[:, bk, nk - 128:nk], cm, ALU.add), t, *sf)
        if qb:
            k1 = V(lambda: vec.tensor_copy(Sm[:, 0:128], PS[:, bk, 0:128]), t)
        sB.done(bi, k1)
        k1 = V(lambda: vec.tensor_reduce(s4[:, 0:1], Sm[:, 0:nk], AX, ALU.max), k1, V.now(), *tf)
        k1 = V(lambda: vec.tensor_scalar(s4[:, 1:2], s4[:, 0:1], -SC2, None, ALU.mult), k1)
        k1 = A(lambda: act.activation(Sm[:, 0:nk], Sm[:, 0:nk], ACT.Exp, bias=s4[:, 1:2], scale=SC2,
                                      accum_out=s4[:, 2:3]), k1)
        live[u] = (si, Sm, ti, s4, k1)

    def scale2(u):
        h, qb = units[u]
        nk = 128 * (qb + 1)
        si, Sm, ti, s4, k1 = live[u]
        k1 = V(lambda: vec.reciprocal(s4[:, 3:4], s4[:, 2:3]), k1)
        k1 = V(lambda: vec.tensor_scalar(Sm[:, 0:nk], Sm[:, 0:nk], s4[:, 3:4], None, ALU.mult), k1)
        stt.done(ti, k1)
        live[u] = (si, Sm, k1)

    def turn2(u):
        h, qb = units[u]
        si, Sm, k1 = live[u]
        bi, bk, fr = tB.take()
        T.wait(k1, *fr)
        for j in range(qb + 1):
            t = T(lambda: tns.transpose(PS[:, bk, j * 128:(j + 1) * 128], Sm[:, j * 128:(j + 1) * 128], ident))
        sS.done(si, t)
        ti, Pt, tf = pT.take()
        nk = 128 * (qb + 1)
        k2 = A(lambda: act.copy(Pt[:, 0:nk], PS[:, bk, 0:nk]), t, *tf)
        tB.done(bi, k2)
        live[u] = (ti, Pt, k2)

    def values2(u):
        h, qb = units[u]
        ti, Pt, k2 = live[u]
        bi, bk, fr = oB.take()
        T.wait(k2, *fr)
        for j in range(qb + 1):
            t = mm(PS[:, bk, 0:128], va[:, j, h * 128:(h + 1) * 128], Pt[:, j * 128:(j + 1) * 128], j == 0, j == qb,
                   inc=(j == qb))
        pT.done(ti, t)
        sl = slice(qb * 128, (qb + 1) * 128)
        oB.done(bi, V(lambda: vec.tensor_tensor(oT[:, h, sl], PS[:, bk, 0:128], zT[:, h, sl], ALU.mult), t))

    for s in range(len(units) + 3):
        for stage, lag in ((scores2, 0), (scale2, 1), (turn2, 2), (values2, 3)):
            if 0 <= s - lag < len(units):
                stage(s - lag)
    fence()
    kg = gate_rows(mod2[0][:, 16:24], [6, 7], None)
    k_y = rows_out("mout", oT, 8, YB, (kg,))
    residual_ln(4, k_ln, YB, (k_y, kg))
    if dbg is not None and upto == 4:
        return dump()

    make_hT(mod2[1][:, 8:16], mod2[1][:, 0:8], [0, 1, 2, 3])
    k_ln = load_ln(5)
    ar = Arena()
    Y = ar.get(6144, "p (n t) -> p n t", n=24)
    SQ = ar.get(4096)
    Z = ar.get(2048, "p (t e) -> p t e", t=2)
    KN = ar.get(2048, "p (n e) -> p n e", n=16)
    VB = ar.get(2048, "p (n e) -> p n e", n=16)
    Lm = ar.get(2048, "p (n e) -> p n e", n=16)
    LT = ar.get(2048, "p (n e) -> p n e", n=16)
    Xm = ar.get(2048, "p (n e) -> p n e", n=16)
    Ym = ar.get(2048, "p (n e) -> p n e", n=16)
    gc0 = CONST_AT["utri"][0]
    GC = ar.get(CONST_AT["gdn_end"][0] - gc0)
    cvs = Slots([ar.get(260)[:, 0:259] for _ in range(4)])
    EG = ar.get(16)
    k_gc = fetch(GC, cst_d[:, gc0:CONST_AT["gdn_end"][0]], T.now(), V.now(), A.now())

    def gc(name):
        a, n = CONST_AT[name]
        return GC[:, a - gc0:a - gc0 + n]

    for c in cvs.items:
        k_z = V(lambda: vec.memset(c[:, 0:3], 0.0))
    cw = prm("conv").rearrange("p (n j) -> p n j", j=4)
    pb = Slots(range(8))
    for n in range(12):
        i, slot, k = weight("gin", n)
        wt = slot.rearrange("p (c f) -> p c f", c=8)
        for b in range(2):
            nb = 2 * n + b
            bi, bk, fr = pb.take()
            T.wait(*fr)
            t = projT(wt, b, hT, PS[:, bk, 0:256], k)
            ci, cv, cf = cvs.take()
            k1 = A(lambda: act.copy(cv[:, 3:259], PS[:, bk, 0:256]), t, *cf)
            pb.done(bi, k1)
            y = Y[:, nb, :]
            k2 = V(lambda: vec.tensor_scalar(y, cv[:, 3:259], cw[:, nb, 3:4], None, ALU.mult), k1, k_z)
            for j in (2, 1, 0):
                k2 = V(lambda: vec.scalar_tensor_tensor(y, cv[:, j:j + 256], cw[:, nb, j:j + 1], y, ALU.mult, ALU.add),
                       k2)
            cvs.done(ci, k2)
            k_sil = A(lambda: act.activation(y, y, ACT.Silu), k2)
        release(i, t)
    for n in range(4):
        i, slot, k = weight("gin", 12 + n)
        wt = slot.rearrange("p (c f) -> p c f", c=8)
        for tb in range(2):
            bi, bk, fr = pb.take()
            T.wait(*fr)
            t = projR(wt, hT, tb, PS[:, bk, 0:256], k)
            pb.done(bi, A(lambda: act.activation(Z[:, tb, n * 256:(n + 1) * 256], PS[:, bk, 0:256], ACT.Silu), t))
        release(i, t)
    i, slot, k = weight("gab", 0)
    wt = slot[:, 0:128].rearrange("p (c f) -> p c f", c=8)
    fence()
    for tb in range(2):
        t = projR(wt, hT, tb, PS[:, 0, tb * 16:tb * 16 + 16], k)
    release(i, t)
    xa, ga, be, gcm = SM[:, 0:16], SM[:, 16:32], SM[:, 32:48], TMP[:, 0:16]
    sp1, sp2 = TMP[:, 16:32], TMP[:, 32:48]
    ea = TMP[:, 48:56]
    ab = PS[:, 0, 0:32].rearrange("p (t s h) -> p t s h", t=2, s=2)
    c3 = lambda ap: ap.rearrange("p (t h) -> p t h", t=2)
    k1 = V(lambda: vec.tensor_tensor(c3(xa), ab[:, :, 0, :], row("dt").unsqueeze(1).to_broadcast([128, 2, 8]),
                                     ALU.add), t)
    k2 = A(lambda: act.activation(c3(be), ab[:, :, 1, :], ACT.Sigmoid), k1)
    k1 = V(lambda: vec.scalar_tensor_tensor(sp1, xa, -1.0, xa, ALU.mult, ALU.max), k1)
    k3 = A(lambda: act.activation(sp2, sp1, ACT.Exp, scale=-1.0), k1)
    k3 = A(lambda: act.activation(sp2, sp2, ACT.Ln, bias=1.0), k3)
    k4 = V(lambda: vec.tensor_scalar(xa, xa, 0.0, None, ALU.max), k1)
    k4 = V(lambda: vec.tensor_tensor(xa, xa, sp2, ALU.add), k3, k4)
    k5 = A(lambda: act.activation(ea, row("alog"), ACT.Exp))
    k4 = V(lambda: vec.tensor_tensor(c3(xa), c3(xa), ea.unsqueeze(1).to_broadcast([128, 2, 8]), ALU.mult), k4, k5)
    k_g = V(lambda: vec.tensor_scalar(ga, xa, -1.0, None, ALU.mult), k4)
    T.wait(k_gc)
    t = mm(PS[:, 1, 0:16], gc("utri"), ga, True, True, k_g, inc=True)
    k_gcm = V(lambda: vec.tensor_copy(gcm, PS[:, 1, 0:16]), t)
    q16 = Y[:, 0:16, :].rearrange("p n t -> p (n t)")
    k1 = A(lambda: act.activation(SQ, q16, ACT.Square))
    for q in range(8):
        bk = 2 + q % 4
        T.wait(V.now())
        t = mm(PS[:, bk, :], ones, SQ[:, q * 512:(q + 1) * 512], True, True, k1, inc=True)
        sl = SQ[:, q * 512:(q + 1) * 512]
        k2 = V(lambda: vec.tensor_scalar(sl, PS[:, bk, :], 1e-6, None, ALU.add), t)
    k2 = A(lambda: act.sqrt(SQ, SQ), k2)
    k2 = V(lambda: vec.reciprocal(SQ, SQ), k2)
    k2 = V(lambda: vec.scalar_tensor_tensor(q16[:, 0:2048], q16[:, 0:2048], 128.0 ** -0.5, SQ[:, 0:2048], ALU.mult,
                                            ALU.mult), k2)
    k2 = V(lambda: vec.tensor_tensor(q16[:, 2048:4096], q16[:, 2048:4096], SQ[:, 2048:4096], ALU.mult), k2)
    fence()
    V.wait(k_gc)
    D = SQ[:, 0:2048].rearrange("p (n e) -> p n e", n=16)
    DT = SQ[:, 2048:4096].rearrange("p (n e) -> p n e", n=16)
    gr = TMP[:, 1024:2048].rearrange("p (n e) -> p n e", n=8)
    GE = GR[:, :].rearrange("p (n e) -> p n e", n=8)
    last = None
    glast = SM[:, 0:8]
    for c in range(2):
        for hh in range(2):
            k1 = None
            for h4 in range(4):
                n = c * 8 + hh * 4 + h4
                k1 = V(lambda: vec.tensor_scalar(gr[:, hh * 4 + h4, :], ones, ga[:, n:n + 1], None, ALU.mult),
                       last)
            bk = 2 * c + hh
            for h4 in range(4):
                t = mm(PS[:, bk, h4 * 128:(h4 + 1) * 128], gr[:, hh * 4 + h4, :], gc("utri"), True, True, k1,
                       inc=True)
            last = t
            for h4 in range(4):
                n = c * 8 + hh * 4 + h4
                src = PS[:, bk, h4 * 128:(h4 + 1) * 128]
                V(lambda: vec.scalar_tensor_tensor(D[:, n, :], src, gcm[:, n:n + 1], gc("mD"), ALU.subtract, ALU.add),
                  t)
                V(lambda: vec.scalar_tensor_tensor(DT[:, n, :], src, gcm[:, n:n + 1], gc("mDT"), ALU.subtract, ALU.add))
            if c == 0:
                V(lambda: vec.tensor_copy(glast[:, hh * 4:hh * 4 + 4],
                                          PS[:, bk, :].rearrange("p (n e) -> p n e", n=4)[:, :, 127]), t)
            else:
                A(lambda: act.activation(GE[:, hh * 4:hh * 4 + 4, :],
                                         PS[:, bk, :].rearrange("p (n e) -> p n e", n=4), ACT.Exp), V.now())
    kd = V.now()
    A(lambda: act.activation(D, D, ACT.Exp, scale=-1.0), kd)
    A(lambda: act.activation(DT, DT, ACT.Exp), kd)
    fence()
    k1 = V(lambda: vec.tensor_tensor(EG[:, 0:8], glast, gcm[:, 0:8], ALU.subtract))
    k1 = A(lambda: act.activation(EG[:, 0:8], EG[:, 0:8], ACT.Exp), k1)
    k2 = A(lambda: act.activation(EG[:, 8:16], gcm[:, 8:16], ACT.Exp))
    pb = Slots(range(4))
    for c in range(2):
        for hh in range(2):
            for kind in range(2):
                bi, bk, fr = pb.take()
                T.wait(*fr)
                for h4 in range(4):
                    h = hh * 4 + h4
                    t = T(lambda: tns.transpose(PS[:, bk, h4 * 128:(h4 + 1) * 128],
                                                Y[:, 8 + 8 * kind + h, c * 128:(c + 1) * 128], ident))
                dst = (KN, VB)[kind][:, c * 8 + hh * 4:c * 8 + hh * 4 + 4, :]
                pb.done(bi, A(lambda: act.copy(dst, PS[:, bk, :].rearrange("p (n e) -> p n e", n=4)), t))
    kr = A.now()
    pb = Slots([4, 5, 6, 7])
    for c in range(2):
        for hh in range(2):
            bi, bk, fr = pb.take()
            T.wait(*fr)
            for h4 in range(4):
                h = hh * 4 + h4
                kt = Y[:, 8 + h, c * 128:(c + 1) * 128]
                t = mm(PS[:, bk, h4 * 128:(h4 + 1) * 128], kt, kt, True, True, inc=True)
            for h4 in range(4):
                n = c * 8 + hh * 4 + h4
                kl = V(lambda: vec.scalar_tensor_tensor(Lm[:, n, :], PS[:, bk, h4 * 128:(h4 + 1) * 128],
                                                        be[:, n:n + 1], D[:, n, :], ALU.mult, ALU.mult), t)
            pb.done(bi, kl)
    for c in range(2):
        for hh in range(2):
            bi, bk, fr = pb.take()
            T.wait(kl, *fr)
            for h4 in range(4):
                n = c * 8 + hh * 4 + h4
                t = T(lambda: tns.transpose(PS[:, bk, h4 * 128:(h4 + 1) * 128], Lm[:, n, :], ident))
            n0 = c * 8 + hh * 4
            k1 = A(lambda: act.copy(LT[:, n0:n0 + 4, :], PS[:, bk, :].rearrange("p (n e) -> p n e", n=4)), t)
            pb.done(bi, k1)
    b16 = lambda ap: ap.unsqueeze(1).to_broadcast([128, 16, 128])
    k2 = V(lambda: vec.tensor_tensor(Xm, Lm, b16(gc("m1")), ALU.mult), kl)
    k2 = V(lambda: vec.tensor_tensor(Xm, b16(ident), Xm, ALU.subtract), k2)
    k3 = V(lambda: vec.tensor_tensor(Ym, LT, b16(gc("mt1")), ALU.mult), k1)
    k3 = V(lambda: vec.tensor_tensor(Ym, b16(ident), Ym, ALU.subtract), k3)
    for n in range(16):
        V(lambda: vec.tensor_scalar(VB[:, n, :], VB[:, n, :], be[:, n:n + 1], None, ALU.mult), kr)
    k1 = V(lambda: vec.tensor_tensor(be[:, 8:16], be[:, 8:16], EG[:, 8:16], ALU.mult), A.now(), V.now())
    k1 = V(lambda: vec.tensor_scalar(EG[:, 8:16], be[:, 8:16], -1.0, None, ALU.mult), k1)
    for n in range(16):
        V(lambda: vec.tensor_scalar(KN[:, n, :], KN[:, n, :], EG[:, n:n + 1], None, ALU.mult), k1)
    fence()
    NT = TMP[:, :].rearrange("p (n e) -> p n e", n=16)
    for c in range(2):
        for hh in range(2):
            bi, bk, fr = pb.take()
            T.wait(*fr)
            for h4 in range(4):
                h = hh * 4 + h4
                t = mm(PS[:, bk, h4 * 128:(h4 + 1) * 128], Y[:, 8 + h, c * 128:(c + 1) * 128],
                       Y[:, h, c * 128:(c + 1) * 128], True, True, inc=True)
            n0 = c * 8 + hh * 4
            kl = V(lambda: vec.tensor_tensor(Lm[:, n0:n0 + 4, :], PS[:, bk, :].rearrange("p (n e) -> p n e", n=4),
                                             DT[:, n0:n0 + 4, :], ALU.mult), t)
            pb.done(bi, kl)
    kq = V(lambda: vec.tensor_tensor(Y[:, 0:8, 128:256], Y[:, 0:8, 128:256], GE, ALU.mult), A.now(), T.now())
    fence()
    TT = SQ[:, 0:2048].rearrange("p (n e) -> p n e", n=16)
    for b in (2, 4, 8, 16, 32, 64):
        k1 = V(lambda: vec.tensor_tensor(NT, LT, b16(gc(f"mt{b}")), ALU.mult), T.now(), V.now())
        kx = []
        for q in range(4):
            for r in range(4):
                n = 4 * q + r
                t = mm(PS[:, q, r * 128:(r + 1) * 128], NT[:, n, :], Xm[:, n, :], True, True, k1, inc=(r == 3))
            kx.append(A(lambda: act.copy(TT[:, 4 * q:4 * q + 4, :], PS[:, q, :].rearrange("p (n e) -> p n e", n=4)), t))
        ts = []
        for q in range(4):
            for r in range(4):
                n = 4 * q + r
                if b < 64:
                    mm(PS[:, 4 + q % 2, r * 128:(r + 1) * 128], Ym[:, n, :], TT[:, n, :], True, True, kx[q],
                       *([ts[q - 2]] if q > 1 else []))
            for r in range(4):
                n = 4 * q + r
                t = mm(PS[:, 6 + q % 2, r * 128:(r + 1) * 128], TT[:, n, :], Ym[:, n, :], True, True, kx[q],
                       *([ts[q - 2]] if q > 1 else []), inc=(r == 3))
            sl = slice(4 * q, 4 * q + 4)
            if b < 64:
                V(lambda: vec.tensor_tensor(Xm[:, sl, :], Xm[:, sl, :],
                                            PS[:, 4 + q % 2, :].rearrange("p (n e) -> p n e", n=4), ALU.subtract), t)
            ts.append(V(lambda: vec.tensor_tensor(Ym[:, sl, :], Ym[:, sl, :],
                                                  PS[:, 6 + q % 2, :].rearrange("p (n e) -> p n e", n=4),
                                                  ALU.subtract), t))
        T.wait(ts[-1])
    fence()
    b4 = lambda bk: PS[:, bk, :].rearrange("p (n e) -> p n e", n=4)
    for hh in range(2):
        for r in range(4):
            h = 4 * hh + r
            t = mm(PS[:, hh, r * 128:(r + 1) * 128], Ym[:, h, :], VB[:, h, :], True, True, inc=True)
        A(lambda: act.copy(TT[:, 4 * hh:4 * hh + 4, :], b4(hh)), t)
        for r in range(4):
            h = 4 * hh + r
            t = mm(PS[:, 2 + hh, r * 128:(r + 1) * 128], KN[:, 8 + h, :], Ym[:, 8 + h, :], True, True, inc=True)
        V(lambda: vec.tensor_copy(NT[:, 4 * hh:4 * hh + 4, :], b4(2 + hh)), t)
    fence()
    for hh in range(2):
        for r in range(4):
            h = 4 * hh + r
            t = mm(PS[:, 4 + hh, r * 128:(r + 1) * 128], KN[:, h, :], TT[:, h, :], True, True, inc=True)
        A(lambda: act.copy(NT[:, 8 + 4 * hh:12 + 4 * hh, :], b4(4 + hh)), t)
    fence()
    OO = KN.rearrange("p (t n) e -> p t (n e)", t=2)
    for hh in range(2):
        for r in range(4):
            h = 4 * hh + r
            mm(PS[:, hh, r * 128:(r + 1) * 128], Ym[:, 8 + h, :], VB[:, 8 + h, :], True, False)
            t = mm(PS[:, hh, r * 128:(r + 1) * 128], NT[:, h, :], NT[:, 8 + h, :], False, True, inc=True)
        A(lambda: act.copy(TT[:, 8 + 4 * hh:12 + 4 * hh, :], b4(hh)), t)
    fence()
    for hh in range(2):
        for r in range(4):
            h = 4 * hh + r
            t = mm(PS[:, 2 + hh, r * 128:(r + 1) * 128], Lm[:, h, :], TT[:, h, :], True, True, inc=True)
        V(lambda: vec.tensor_copy(KN[:, 4 * hh:4 * hh + 4, :], b4(2 + hh)), t)
        for r in range(4):
            h = 4 * hh + r
            mm(PS[:, 4 + hh, r * 128:(r + 1) * 128], Lm[:, 8 + h, :], TT[:, 8 + h, :], True, False)
            t = mm(PS[:, 4 + hh, r * 128:(r + 1) * 128], Y[:, h, 128:256], NT[:, 8 + h, :], False, True, inc=True)
        V(lambda: vec.tensor_copy(KN[:, 8 + 4 * hh:12 + 4 * hh, :], b4(4 + hh)), t)
    fence()
    k1 = head_norm(OO, row("nw"), 1.0, 1e-6)
    k1 = V(lambda: vec.tensor_tensor(OO, OO, Z, ALU.mult), k1)
    oT = Lm.rearrange("p n e -> p (n e)").rearrange("p (h t) -> p h t", h=8)
    k1 = rows_to_T(OO, oT, 8, [4, 5, 6, 7], k1)
    fence()
    kg = gate_rows(mod2[1][:, 16:24], [6, 7], None)
    k_y = rows_out("gout", oT, 8, YB, (kg,))
    k1 = residual_ln(5, k_ln, YB, (k_y, kg))
    s = sem("out")
    S.wait(k1)
    syn.dma_start(out_d.rearrange("(t p) d -> p t d", p=128), xs).then_inc(s, 16)
    syn.wait_ge(s, 16)


def cols_items(wm, width=256):
    kk, n = wm.shape
    return wm.reshape(kk // 128, 128, n // width, width).transpose(2, 1, 0, 3).reshape(n // width, 128, -1)


def half_items(wm):
    kk = wm.shape[0]
    return wm.reshape(kk // 512, 4, 128, 2, 512).transpose(3, 0, 2, 1, 4).reshape(-1, 128, 2048)


def column(v):
    return v.reshape(-1, 128).T


def kernel(**a):
    import concourse.bacc as bacc
    from concourse.bass_utils import run_bass_kernel_spmd as run

    a = {k: np.asarray(v) for k, v in a.items()}
    nc = bacc.Bacc("TRN2", target_bir_lowering=False, num_devices=1)
    arrays, r = prepare(a, nc)
    nc_out = nc.dram_tensor("out", (256, 1024), F, kind="ExternalOutput").ap()
    build(nc, *r, nc_out)
    res = run(nc, [arrays], core_ids=[0])
    return res.results[0]["out"].reshape(1, 256, 1024)


def prepare(a, nc):
    arrays = {}

    def give(name, x):
        x = np.ascontiguousarray(x)
        arrays[name] = x
        return nc.dram_tensor(name, x.shape, F, kind="ExternalInput").ap()

    cst = constants()
    w = {}
    for l in range(2):
        w[f"ada{l}"] = give(f"w_ada{l}", cols_items(a["ada_w"][l]))
        w[f"ad2{l}"] = give(f"w_ad2{l}", cols_items(a["ada_w_2"][l]))
        w[f"wq{l}"] = give(f"w_wq{l}", cols_items(a["peer_wq"][l]))
        w[f"keys{l}"] = give(f"w_keys{l}", a["peer_keys"][l].reshape(16, 128, 128).transpose(2, 0, 1).reshape(1, 128, 2048))
        uv = np.empty((128, 128, 2, 1024), np.float32)
        uv[:, :, 0, :] = a["peer_u"][l].reshape(128, 128, 8, 128).transpose(1, 3, 2, 0).reshape(128, 128, 1024)
        uv[:, :, 1, :] = a["peer_v"][l].reshape(128, 128, 1024).transpose(1, 0, 2)
        w[f"uv{l}"] = give(f"w_uv{l}", uv.reshape(128, 128, 2048))
    w["abin"] = give("w_abin", cols_items(a["ab_w_in"][0]))
    w["about"] = give("w_about", half_items(a["ab_w_out"][0]))
    w["pin"] = give("w_pin", cols_items(a["pool_w_in"][0]))
    w["pgrp"] = give("w_pgrp", a["pool_w_grp"][0].reshape(4, 2, 128, 256).transpose(2, 0, 1, 3).reshape(1, 128, 2048))
    w["pout"] = give("w_pout", half_items(a["pool_w_out"][0]))
    w["min"] = give("w_min", cols_items(a["moba_w_in_2"][0]))
    w["mout"] = give("w_mout", half_items(a["moba_w_out_2"][0]))
    w["gin"] = give("w_gin", cols_items(a["gdn_w_in_2"][0][:, :4096]))
    w["gab"] = give("w_gab", cols_items(a["gdn_w_in_2"][0][:, 4096:], 16))
    w["gout"] = give("w_gout", half_items(a["gdn_w_out_2"][0]))
    prm = np.concatenate([
        column(a["c"][0]), column(a["c_ctx"]), column(a["c_2"][0]),
        column(a["ada_b"][0]), column(a["ada_b"][1]), column(a["ada_b_2"][0]), column(a["ada_b_2"][1]),
        a["sgu_b"][0].T, column(a["pool_scale"][0]),
        a["gdn_conv_w_2"][0].reshape(4, 24, 128).transpose(2, 1, 0).reshape(128, 96)], 1)
    rows = np.concatenate([
        a["diff_lam"][0].reshape(-1), a["diff_norm_g"][0], a["sgu_ln_g"][0], a["sgu_ln_b"][0],
        a["gdn_a_log_2"][0], a["gdn_dt_bias_2"][0], a["gdn_norm_w_2"][0]])
    lns = np.stack([v for l in range(2) for n in range(2) for v in (a["ln_g"][l, n], a["ln_b"][l, n])]
                   + [v for l in range(2) for v in (a["ln_g_2"][l], a["ln_b_2"][l])])
    r = (w, give("cst", cst), give("prm", prm), give("rows", rows), give("x", a["x"][0]), give("xT", a["x"][0].T),
         give("cT", a["ctx"][0].T), give("sguw", a["sgu_w"][0].transpose(2, 0, 1).reshape(128, 512)),
         give("lns", lns))
    return arrays, r
```

```python
import math
import numpy as np
import concourse.bass as bass
from concourse import mybir

F = mybir.dt.float32
U32 = mybir.dt.uint32
ALU = mybir.AluOpType
ACT = mybir.ActivationFunctionType
AX = mybir.AxisListType.X
NEG = -1e30
ALPHA = 4.0 ** 0.25
F16 = mybir.dt.float16
R = mybir.dt.float32r
RING = 4
NPART = 4
PW = 128 // NPART
GT = 256 // PW
GSCALE = 2.0 ** 14
LEAD = 22

CONST_AT = {}


def constants():
    p = np.arange(128)
    cols = []

    def put(name, a):
        CONST_AT[name] = (sum(x.shape[1] for x in cols), a.shape[1])
        cols.append(a.astype(np.float32))

    eye = np.eye(128)
    put("ident", eye)
    put("ones", np.ones((128, 128)))
    put("iota", np.broadcast_to(p[None, :], (128, 128)))
    put("iota16", np.broadcast_to(np.arange(16)[None, :], (128, 16)))
    put("persist_end", np.zeros((128, 0)))
    t = np.arange(256)
    inv = 10000.0 ** (-np.arange(16, dtype=np.float32) / 16)
    ang = np.concatenate([(t // 64)[:, None] * inv, (t % 64)[:, None] * inv], -1).astype(np.float32)
    put("cos", np.cos(ang).T[p % 32])
    put("sin", np.sin(ang).T[p % 32])
    perm = np.zeros((128, 128))
    for m in range(128):
        if m % 64 < 32:
            perm[m + 32, m] = -1.0
        else:
            perm[m - 32, m] = 1.0
    put("perm", perm)
    put("rope_end", np.zeros((128, 0)))
    pool = np.zeros((2, 128, 4, 256))
    for g, w in enumerate((2, 4, 8, 16)):
        for q in range(256):
            lo, hi = max(q - w // 2, 0), min(q + w - w // 2, 256)
            for s in range(lo, hi):
                pool[s // 128, s % 128, g, q] += 1.0 / (hi - lo)
            pool[q // 128, q % 128, g, q] -= 1.0
    put("pool", pool.transpose(1, 0, 2, 3).reshape(128, 2048))
    i, j = p[:, None], p[None, :]
    put("causal", np.where(j <= i, 0.0, NEG))
    put("utri", (i <= j) * 1.0)
    put("mD", np.where(j > i, -NEG, 0.0))
    put("mDT", np.where(j < i, NEG, 0.0))
    for b in (1, 2, 4, 8, 16, 32, 64):
        m = (i // (2 * b) == j // (2 * b)) & (i % (2 * b) >= b) & (j % (2 * b) < b)
        if b == 1:
            put("m1", m * 1.0)
        put(f"mt{b}", m.T * 1.0)
    put("gdn_end", np.zeros((128, 0)))
    return np.ascontiguousarray(np.concatenate(cols, 1))


PRM = [("ab0", 48), ("ab1", 48), ("a20", 24), ("a21", 24),
       ("sgub", 4), ("psc", 8), ("conv", 96)]
ROWS = [("lam", 256), ("dng", 128), ("alog", 8), ("dt", 8), ("nw", 128), ("kept_end", 0), ("sg", 512), ("sb", 512)]


def offsets(table):
    at, out = 0, {}
    for name, w in table:
        out[name] = (at, w)
        at += w
    return out, at


PRM_AT, PRM_N = offsets(PRM)
ROW_AT, ROW_N = offsets(ROWS)

def experts_and(layer, extra):
    out, extra = [(f"up{layer}", n) for n in range(LEAD // 2)], list(extra)
    for n in range(128 - LEAD):
        out.append((f"uv{layer}", n))
        if n % 4 == 3 and extra:
            out.append(extra.pop(0))
    assert not extra
    return out + [(f"down{layer}", n) for n in range(LEAD // 2)]


STREAM = ([("ada0", n) for n in range(8)] + [("abin", 0), ("abin", 1)]
          + [x for n in range(2, 16) for x in (("abin", n), ("ada0", 6 + n))] + [("ada0", 22), ("ada0", 23)]
          + [("about", n) for n in range(6)] + [("keys0", 0)] + [("wq0", n) for n in range(8)]
          + experts_and(0, [("ada1", n) for n in range(24)])
          + [("pin", n) for n in range(4)] + [("pgrp", 0)] + [("pout", n) for n in range(4)]
          + [("keys1", 0)] + [("wq1", n) for n in range(8)]
          + experts_and(1, [("ad20", n) for n in range(12)] + [("ad21", n) for n in range(12)])
          + [("min", n) for n in range(16)] + [("mout", n) for n in range(4)]
          + [("gab", 0)] + [("gin", n) for n in range(16)] + [("gout", n) for n in range(4)])


class Engine:

    def __init__(self, eng, sem):
        self.eng, self.sem, self.count, self.seen = eng, sem, 0, {}

    def wait(self, *tokens):
        for t in tokens:
            if t is None:
                continue
            sem, value = t
            if self.seen.get(sem.name, 0) < value:
                self.seen[sem.name] = value
                self.eng.wait_ge(sem, value)

    def __call__(self, make, *tokens):
        self.wait(*tokens)
        make().then_inc(self.sem, 1)
        self.count += 1
        return (self.sem, self.count)

    def quiet(self, make, *tokens):
        self.wait(*tokens)
        make()

    def now(self):
        return (self.sem, self.count)


class Slots:

    def __init__(self, items):
        self.items, self.free, self.n = list(items), {}, 0

    def take(self):
        i = self.n % len(self.items)
        self.n += 1
        return i, self.items[i], self.free.get(i, ())

    def done(self, i, *tokens):
        self.free[i] = tokens


def build(nc, w, cst_d, prm_d, rows_d, cnd_d, x_d, xT_d, cT_d, sguw_d, lng_d, out_d, upto=99, dbg=None):
    tns, vec, act, gps, syn = nc.tensor, nc.vector, nc.scalar, nc.gpsimd, nc.sync
    nsem = [0, 0]

    def sem(name):
        nsem[0] += 1
        return nc.alloc_semaphore(name)

    T, V, A, G = Engine(tns, sem("pe")), Engine(vec, sem("dve")), Engine(act, sem("act")), Engine(gps, sem("pool"))
    S = Engine(syn, sem("sp"))

    def sb(name, n):
        return nc.alloc_sbuf_tensor(name, [128, n], F)

    ring = sb("ring", RING * 2048)
    XS = sb("XS", 2048)
    HT = sb("HT", 2048)
    TMP = sb("TMP", 2048)
    GR = sb("GR", 1024)
    LN = sb("LN", 2048)
    CP = sb("CP", CONST_AT["persist_end"][0])
    PR = sb("PR", PRM_N)
    RW = sb("RW", ROW_AT["kept_end"][0])
    MOD = sb("MOD", 48 + 16 + 48 + 48)
    SM = sb("SM", 64)
    CR = sb("CR", 1024)
    PS = nc.alloc_psum_tensor("PS", [128, 8, 512], F)

    xs = XS[:, :].rearrange("p (t d) -> p t d", t=2)
    tmp = TMP[:, :].rearrange("p (t d) -> p t d", t=2)
    hT = HT[:, :].rearrange("p (c t) -> p c t", c=8)
    lng, lnb = LN[:, 0:1024], LN[:, 1024:2048]

    def cp(name):
        a, n = CONST_AT[name]
        return CP[:, a:a + n]

    ident, ones, iota, iota16 = cp("ident"), cp("ones"), cp("iota"), cp("iota16")

    def prm(name):
        a, n = PRM_AT[name]
        return PR[:, a:a + n]

    def row(name):
        a, n = ROW_AT[name]
        return RW[:, a:a + n]

    class Arena:

        def __init__(self):
            self.open = []

        def get(self, size, dims=None, dt=F, **k):
            nsem[1] += 1
            g = nc.sbuf_tensor(f"st{nsem[1]}", [128, size], dt)
            self.open.append(g)
            ap = g.__enter__()[:, :]
            return ap.rearrange(dims, **k) if dims else ap

        def close(self):
            while self.open:
                self.open.pop().__exit__(None, None, None)

    def fence():
        now = [e.now() for e in (T, V, A, G) if e.count]
        for e in (T, V, A, G):
            e.wait(*now)

    def fetch(dst, src, *tokens, name=None):
        s = sem(f"ld{nsem[0]}")
        G.wait(*tokens)
        gps.dma_start(dst, src).then_inc(s, 16)
        return (s, 16)

    wsem = [sem(f"w{i}") for i in range(RING)]
    loaded = [0]
    released = {}

    def issue():
        n = loaded[0]
        if n >= len(STREAM):
            return
        kind, i = STREAM[n]
        slot = n % RING
        if n >= RING:
            S.wait(*released[n - RING])
        src = w[kind][i]
        syn.dma_start(ring[:, slot * 2048:slot * 2048 + src.shape[1]], src).then_inc(wsem[slot], 16)
        loaded[0] += 1

    used = [0]

    def weight(kind, i):
        n = used[0]
        assert STREAM[n] == (kind, i), (STREAM[n], kind, i)
        used[0] += 1
        if n == 0:
            for _ in range(RING):
                issue()
        slot = n % RING
        return n, ring[:, slot * 2048:(slot + 1) * 2048], (wsem[slot], 16 * (n // RING + 1))

    def release(n, *tokens):
        released[n] = tokens
        while loaded[0] - RING in released and loaded[0] < len(STREAM):
            issue()

    def mm(out, lhsT, rhs, start, stop, *tokens, inc=False):
        f = lambda: tns.matmul(out, lhsT, rhs, start=start, stop=stop)
        return T(f, *tokens) if inc else T.quiet(f, *tokens)

    CCR = GR[:, :]
    k_cc = [fetch(CR[:, :], cnd_d[0].partition_broadcast(128)), fetch(CCR, cnd_d[1].partition_broadcast(128))]
    k_c = fetch(CP[:, :], cst_d[:, 0:CONST_AT["persist_end"][0]])
    k_p = fetch(PR[:, :], prm_d)
    k_r = fetch(RW[:, :], rows_d[0:ROW_AT["kept_end"][0]].partition_broadcast(128))

    mod0, modc, mod1 = MOD[:, 0:48], MOD[:, 48:64], MOD[:, 64:112]
    mod2 = [MOD[:, 112:136], MOD[:, 136:160]]

    def ada(kind, n, cond, cols, cond2=None, cols2=None, junk=None):
        i, slot, k = weight(kind, n)
        V.wait(k)
        t = None
        for b in range(2):
            wt = slot[:, b * 1024:(b + 1) * 1024]
            if cond2 is not None:
                V.wait(V.now())
                V(lambda: vec.tensor_tensor_reduce(junk, wt, cond2, 1.0, 0.0, ALU.mult, ALU.add,
                                                   cols2[:, 2 * n + b:2 * n + b + 1]))
            t = V(lambda: vec.tensor_tensor_reduce(wt, wt, cond, 1.0, 0.0, ALU.mult, ALU.add,
                                                   cols[:, 2 * n + b:2 * n + b + 1]))
        release(i, t)
        return t

    def ada_end(cols, bias, scales):
        k = V(lambda: vec.tensor_tensor(cols, cols, bias, ALU.add), V.now())
        for a in scales:
            k = V(lambda: vec.tensor_scalar(cols[:, a:a + 8], cols[:, a:a + 8], 1.0, None, ALU.add), k)
        return k

    def gate_rows(cols, banks, k_cols, k_free=(), work=TMP):
        d = work[:, 0:1024].rearrange("p (c m) -> p c m", c=8)
        k1 = V(lambda: vec.tensor_tensor(d, ident.unsqueeze(1).to_broadcast([128, 8, 128]),
                                         cols.unsqueeze(2).to_broadcast([128, 8, 128]), ALU.mult),
               k_cols, *k_free)
        for b in range(2):
            k2 = mm(PS[:, banks[b], :], ones, work[:, b * 512:(b + 1) * 512], True, True, k1, inc=True)
        for b in range(2):
            k3 = A(lambda: act.copy(GR[:, b * 512:(b + 1) * 512], PS[:, banks[b], :]), k2)
        return k3

    def modulated(dst, sc, sh, src, *tokens):
        for c in range(8):
            s1, s2 = sc[:, c:c + 1], sh[:, c:c + 1]
            t = V(lambda: vec.tensor_scalar(dst[:, c, :], src[:, c, :], s1, s2, ALU.mult, ALU.add), *tokens)
        return t

    def split_cols(src, HH, HL, c0, c1, k):
        a = A(lambda: act.copy(HH[:, c0:c1, :], src[:, c0:c1, :]), k)
        return V(lambda: vec.tensor_tensor(HL[:, c0:c1, :], src[:, c0:c1, :], HH[:, c0:c1, :].bitcast(F),
                                           ALU.subtract), a, k)

    def make_hT(sc, sh, HH, HL):
        V.wait(T.now())
        A.wait(T.now())
        for q in range(4):
            for jj in range(2):
                c = 2 * q + jj
                src = PS[:, q, jj * 256:jj * 256 + 256]
                s1, s2 = sc[:, c:c + 1], sh[:, c:c + 1]
                if q % 2:
                    t = A(lambda: act.activation(hT[:, c, :], src, ACT.Identity, bias=s2, scale=s1))
                else:
                    t = V(lambda: vec.tensor_scalar(hT[:, c, :], src, s1, s2, ALU.mult, ALU.add))
            c = slice(2 * q, 2 * q + 2)
            a = A(lambda: act.copy(HH[:, c, :], hT[:, c, :]), t)
            k = V(lambda: vec.tensor_tensor(HL[:, c, :], hT[:, c, :], HH[:, c, :].bitcast(F), ALU.subtract), a, t)
            T.wait(k)
        return k

    class Splitter:

        def __init__(self, ar, n=2):
            self.HI, self.LO = ar.get(2048 * n, dt=R), ar.get(2048 * n, dt=R)
            self.n = n
            self.slots = Slots(range(n))
            self.ready = []

        def part(self, at, n, src, *tokens, eng=None):
            hi, lo = self.HI[:, at:at + n], self.LO[:, at:at + n]
            a = A(lambda: act.copy(hi, src), *tokens)
            if eng is G:
                b = G(lambda: gps.tensor_tensor(lo, src, hi.bitcast(F), ALU.subtract), a, *tokens)
            else:
                b = V(lambda: vec.tensor_tensor(lo, src, hi.bitcast(F), ALU.subtract), a, *tokens)
            return hi, lo, b

        def item(self, kind, i, eng=None):
            n, slot, k = weight(kind, i)
            si, s, fr = self.slots.take()
            hi, lo, b = self.part(s * 2048, 2048, slot, k, *fr, eng=eng)
            release(n, b)
            return si, hi, lo, b

        def start(self, kind, n):
            self.ready = [self.item(kind, i, G) for i in range(n)]

        def run(self, kind, items, body, eng=None):
            ahead = self.ready + [self.item(kind, i) for i in items[len(self.ready):self.n - 1]]
            self.ready = []
            for m, n in enumerate(items):
                si, hi, lo, b = ahead.pop(0)
                if m + self.n - 1 < len(items):
                    e = (eng if m else None) if eng is None or isinstance(eng, Engine) else eng(m)
                    ahead.append(self.item(kind, items[m + self.n - 1], e))
                T.wait(b)
                self.slots.done(si, body(n, hi, lo))

    def mm3(out, a, b, first, last):
        (ah, al), (bh, bl) = a, b
        mm(out, ah, bh, first, False)
        mm(out, ah, bl, False, False)
        return mm(out, al, bh, False, last, inc=last)

    def projT3(hi, lo, b, HH, HL, out):
        h3, l3 = (z.rearrange("p (c f) -> p c f", c=8) for z in (hi, lo))
        sl = slice(b * 128, (b + 1) * 128)
        for c in range(8):
            t = mm3(out, (h3[:, c, sl], l3[:, c, sl]), (HH[:, c, :], HL[:, c, :]), c == 0, c == 7)
        return t

    def projR3(hi, lo, tb, HH, HL, out):
        h3, l3 = (z.rearrange("p (c f) -> p c f", c=8) for z in (hi, lo))
        sl = slice(tb * 128, (tb + 1) * 128)
        for c in range(8):
            t = mm3(out, (HH[:, c, sl], HL[:, c, sl]), (h3[:, c, :], l3[:, c, :]), c == 0, c == 7)
        return t

    def rows_out3(kind, sp, HH, HL, banks, k_in, k_in1=()):
        T.wait(*k_in)
        tok = []

        def body(n, hi, lo):
            nh, kg = n // 2, n % 2
            h3, l3 = (z.rearrange("p (c f) -> p c f", c=4) for z in (hi, lo))
            for tb in range(2):
                if tb:
                    T.wait(*k_in1)
                sl = slice(tb * 128, (tb + 1) * 128)
                for c in range(4):
                    kc = kg * 4 + c
                    o = PS[:, banks[tb][nh], :]
                    mm(o, HH[:, kc, sl], h3[:, c, :], kc == 0, False)
                    mm(o, HH[:, kc, sl], l3[:, c, :], False, False)
                    t = mm(o, HL[:, kc, sl], h3[:, c, :], False, kc == 7, inc=(c == 3))
                if kg:
                    tok.append(((tb, nh), t))
            return t

        sp.run(kind, list(range(4)), body)
        return tok

    def residual_ln(ln_i, k_ln, banks, k_y, kg, turn=True):
        st = SM[:, 0:24]
        mv = SM[:, 24:28]
        rs, nm = SM[:, 28:30], SM[:, 30:32]
        V.wait(kg)

        def scale(tb, k):
            k = V(lambda: vec.reciprocal(rs[:, tb:tb + 1], rs[:, tb:tb + 1]), k)
            k = V(lambda: vec.tensor_scalar(nm[:, tb:tb + 1], mv[:, 2 * tb:2 * tb + 1], rs[:, tb:tb + 1], -1.0,
                                            ALU.mult, ALU.mult), k)
            k = A(lambda: act.activation(xs[:, tb, :], xs[:, tb, :], ACT.Identity, bias=nm[:, tb:tb + 1],
                                         scale=rs[:, tb:tb + 1]), k)
            if tb == 0:
                return G(lambda: gps.tensor_tensor(xs[:, tb, :], xs[:, tb, :], lng, ALU.mult), k, *k_ln)
            return V(lambda: vec.tensor_tensor(xs[:, tb, :], xs[:, tb, :], lng, ALU.mult), k, *k_ln)

        seen, waiting = [0, 0], None
        for (tb, nh), ky in k_y:
            sl = slice(nh * 512, nh * 512 + 512)
            k1 = V(lambda: vec.tensor_tensor(tmp[:, tb, sl], PS[:, banks[tb][nh], :], GR[:, sl], ALU.mult), ky)
            k1 = V(lambda: vec.scalar_tensor_tensor(xs[:, tb, sl], xs[:, tb, sl], ALPHA, tmp[:, tb, sl],
                                                    ALU.mult, ALU.add), k1)
            o = (tb * 2 + nh) * 6
            if waiting:
                k_0 = scale(*waiting)
                waiting = None
            k1 = V(lambda: vec.bn_stats(st[:, o:o + 6], xs[:, tb, sl]), k1)
            seen[tb] += 1
            if seen[tb] == 2:
                k2 = V(lambda: vec.bn_aggr(mv[:, 2 * tb:2 * tb + 2], st[:, tb * 12:tb * 12 + 12]), V.now())
                k2 = V(lambda: vec.tensor_scalar(rs[:, tb:tb + 1], mv[:, 2 * tb + 1:2 * tb + 2], 1e-5, None, ALU.add),
                       k2)
                waiting = (tb, A(lambda: act.sqrt(rs[:, tb:tb + 1], rs[:, tb:tb + 1]), k2))
        k_1 = scale(*waiting)
        k4 = None
        for tb, k in ((0, k_0), (1, k_1)):
            k4 = V(lambda: vec.tensor_tensor(xs[:, tb, :], xs[:, tb, :], lnb, ALU.add), k, *k_ln)
            if turn:
                T.wait(k4)
                for c in range(8):
                    at = c % 2 * 256 + tb * 128
                    T(lambda: tns.transpose(PS[:, c // 2, at:at + 128], xs[:, tb, c * 128:(c + 1) * 128], ident))
        return k4

    def load_ln(i):
        s = [fetch(LN[:, 1024 * j:1024 * j + 1024], lng_d[2 * i + j:2 * i + j + 1, :].rearrange("a d -> (a d)")
                   .partition_broadcast(128), V.now()) for j in range(2)]
        return s

    def rows_out(kind, lhs, nk, banks, k_in):
        tok = []
        T.wait(*k_in)
        n = 0
        for nh in range(2):
            for kg in range(nk // 4):
                i, slot, k = weight(kind, n)
                n += 1
                wt = slot.rearrange("p (c f) -> p c f", c=4)
                for tb in range(2):
                    for c in range(4):
                        kc = kg * 4 + c
                        t = mm(PS[:, banks[tb][nh], :], lhs[:, kc, tb * 128:(tb + 1) * 128], wt[:, c, :],
                               kc == 0, kc == nk - 1, k, inc=(c == 3))
                    if kg == nk // 4 - 1:
                        tok.append(((tb, nh), t))
                release(i, t)
        return tok

    ar = Arena()
    qT = ar.get(2048, "p (h t) -> p h t", h=8)
    kT = ar.get(4096, "p (h t) -> p h t", h=8)
    va = ar.get(4096, "p (b e) -> p b e", b=4)
    gg = ar.get(2048, "p (t e) -> p t e", t=2)
    hcT = XS[:, :].rearrange("p (c t) -> p c t", c=8)
    rope = ar.get(640)
    sguw = ar.get(512, "p (g q) -> p g q", g=4)
    k1 = A(lambda: act.activation(CR[:, :], CR[:, :], ACT.Silu), k_cc[0])
    k2 = A(lambda: act.activation(CCR, CCR, ACT.Silu), k_cc[1])
    V.wait(k1, k2)
    k_rope = fetch(rope, cst_d[:, CONST_AT["cos"][0]:CONST_AT["rope_end"][0]])
    k_sgw = fetch(sguw, sguw_d)
    cosT, sinT, perm = rope[:, 0:256], rope[:, 256:512], rope[:, 512:640]
    k_xT = fetch(hT, xT_d.rearrange("(c p) t -> p c t", p=128))
    k_cT = fetch(hcT, cT_d.rearrange("(c p) t -> p c t", p=128))
    k_ln = load_ln(0)
    for n in range(8):
        ada("ada0", n, CR[:, :], mod0, CCR, modc, TMP[:, 0:1024])
    V.wait(k_p)
    ada_end(modc, prm("ab0")[:, 0:16], (8,))
    V.wait(k_p)
    k_m = ada_end(mod0[:, 0:16], prm("ab0")[:, 0:16], (8,))
    modulated(hT, mod0[:, 8:16], mod0[:, 0:8], hT, k_m, k_xT)
    k_h = modulated(hcT, modc[:, 8:16], modc[:, 0:8], hcT, k_m, k_cT)

    raws = Slots([ar.get(256) for _ in range(2)])
    tms = Slots([ar.get(256) for _ in range(2)])
    ar2 = Arena()
    sp = Splitter(ar2)
    XH, XL, YH, YL = (ar2.get(2048, "p (c t) -> p c t", dt=R, c=8) for _ in range(4))
    for e in (T, V, A, G):
        e.wait(k_c, k_p, k_r)
    T.wait(split_cols(hT, XH, XL, 0, 8, k_h), split_cols(hcT, YH, YL, 0, 8, k_h))
    k_x = fetch(xs, x_d.rearrange("(t p) d -> p t d", p=128), V.now(), A.now())
    pb = Slots(range(8))
    T.wait(k_h)
    V.wait(k_rope)
    T.wait(k_rope)

    def projT(wt, b, rhs, out, k):
        for c in range(8):
            t = mm(out, wt[:, c, b * 128:(b + 1) * 128], rhs[:, c, :], c == 0, c == 7, k, inc=(c == 7))
        return t

    def projR(wt, lhs, tb, out, k):
        for c in range(8):
            t = mm(out, lhs[:, c, tb * 128:(tb + 1) * 128], wt[:, c, :], c == 0, c == 7, k, inc=(c == 7))
        return t


    def body(n, hi, lo):
        if n:
            ada("ada0", 7 + n, CR[:, :], mod0)
        if n < 8:
            for b in range(2):
                h = (2 * n + b) % 8
                dst = qT[:, h, :] if n < 4 else kT[:, h, 256:512]
                if n >= 4:
                    bi, bk, fr = pb.take()
                    T.wait(*fr)
                    t = projT3(hi, lo, b, YH, YL, PS[:, bk, 0:256])
                    pb.done(bi, A(lambda: act.copy(kT[:, h, 0:256], PS[:, bk, 0:256]), t))
                bi, bk, fr = pb.take()
                T.wait(*fr)
                t = projT3(hi, lo, b, XH, XL, PS[:, bk, 0:256])
                ri, raw, rf = raws.take()
                k1 = A(lambda: act.copy(raw, PS[:, bk, 0:256]), t, *rf)
                turns.append((bi, bk, ri, raw, k1, dst))
                if len(turns) > 1:
                    rotate(*turns.pop(0))
            return t
        if n == 8:
            rotate(*turns.pop(0))
        if n < 12:
            blocks = [(YH, YL, 0, va[:, 0, :]), (YH, YL, 1, va[:, 1, :]), (XH, XL, 0, va[:, 2, :]),
                      (XH, XL, 1, va[:, 3, :])]
            at = (n - 8) * 256
        else:
            blocks = [(XH, XL, 0, gg[:, 0, :]), (XH, XL, 1, gg[:, 1, :])]
            at = (n - 12) * 256
        for sh_, sl_, tb, dst in blocks:
            bi, bk, fr = pb.take()
            T.wait(*fr)
            t = projR3(hi, lo, tb, sh_, sl_, PS[:, bk, 0:256])
            if n < 12:
                e = A(lambda: act.copy(dst[:, at:at + 256], PS[:, bk, 0:256]), t)
            else:
                e = A(lambda: act.activation(dst[:, at:at + 256], PS[:, bk, 0:256], ACT.Gelu_apprx_tanh), t)
            pb.done(bi, e)
        return t

    turns = []

    def rotate(bi, bk, ri, raw, k1, dst):
        t2 = mm(PS[:, bk, 256:512], perm, raw, True, True, k1, inc=True)
        mi, tm, mf = tms.take()
        k2 = V(lambda: vec.tensor_tensor(tm, raw, cosT, ALU.mult), k1, *mf)
        raws.done(ri, t2, k2)
        k3 = V(lambda: vec.tensor_tensor(dst, PS[:, bk, 256:512], sinT, ALU.mult), t2)
        pb.done(bi, k3)
        k4 = V(lambda: vec.tensor_tensor(dst, dst, tm, ALU.add), k2, k3)
        tms.done(mi, k4)

    sp.run("abin", list(range(16)), body, G)
    ada("ada0", 23, CR[:, :], mod0)
    k_mod0 = ada_end(mod0[:, 16:48], prm("ab0")[:, 16:48], (16,))
    fence()
    ar2.close()
    catT = ar.get(3072, "p (c t) -> p c t", c=12)
    sgb = ar.get(1024)
    k_sgb = fetch(sgb, rows_d[ROW_AT["sg"][0]:ROW_N].partition_broadcast(128))

    lam = SM[:, 32:36]
    lr = row("lam").rearrange("p (a b d) -> p a b d", a=2, b=2)
    k1 = V(lambda: vec.tensor_tensor(TMP[:, 0:128].rearrange("p (a d) -> p a d", a=2), lr[:, :, 0, :], lr[:, :, 1, :],
                                     ALU.mult))
    k1 = V(lambda: vec.tensor_reduce(lam[:, 0:2], TMP[:, 0:128].rearrange("p (a d) -> p a d", a=2), AX, ALU.add), k1)
    k1 = A(lambda: act.activation(lam[:, 0:2], lam[:, 0:2], ACT.Exp), k1)
    k1 = V(lambda: vec.tensor_tensor(lam[:, 2:3], lam[:, 0:1], lam[:, 1:2], ALU.subtract), k1)
    lam_init = 0.8 - 0.6 * math.exp(-0.3 * 0)
    k_lam = V(lambda: vec.tensor_scalar(lam[:, 3:4], lam[:, 2:3], lam_init, -1.0, ALU.add, ALU.mult), k1)

    gu, gv = gg[:, :, 0:512], gg[:, :, 512:1024]
    st = SM[:, 0:12]
    mv = SM[:, 24:28]
    m2 = mv.rearrange("p (t s) -> p t s", s=2)
    rs = SM[:, 28:30]
    for tb in range(2):
        k1 = V(lambda: vec.bn_stats(st[:, tb * 6:tb * 6 + 6], gv[:, tb, :]))
        k1 = V(lambda: vec.bn_aggr(mv[:, 2 * tb:2 * tb + 2], st[:, tb * 6:tb * 6 + 6]), k1)
    k1 = V(lambda: vec.tensor_scalar(rs, m2[:, :, 1], 1e-5, None, ALU.add), k1)
    k1 = A(lambda: act.sqrt(rs, rs), k1)
    k1 = V(lambda: vec.reciprocal(rs, rs), k1)
    for tb in range(2):
        k2 = V(lambda: vec.tensor_scalar(gv[:, tb, :], gv[:, tb, :], mv[:, 2 * tb:2 * tb + 1], rs[:, tb:tb + 1],
                                         ALU.subtract, ALU.mult), k1)
        k2 = V(lambda: vec.tensor_tensor(gv[:, tb, :], gv[:, tb, :], sgb[:, 0:512], ALU.mult), k2, k_sgb)
        k2 = V(lambda: vec.tensor_tensor(gv[:, tb, :], gv[:, tb, :], sgb[:, 512:1024], ALU.add), k2)
        T.wait(k_sgw)
        for g in range(4):
            t = mm(PS[:, tb, g * 128:(g + 1) * 128], sguw[:, g, :], gv[:, tb, g * 128:(g + 1) * 128], True, True,
                   k2, inc=(g == 3))
        for g in range(4):
            sl = slice(g * 128, (g + 1) * 128)
            k3 = V(lambda: vec.scalar_tensor_tensor(gu[:, tb, sl], PS[:, tb, sl], prm("sgub")[:, g:g + 1],
                                                    gu[:, tb, sl], ALU.add, ALU.mult), t)
        for g in range(4):
            f = lambda: tns.transpose(PS[:, 2 + tb, g * 128:(g + 1) * 128], gu[:, tb, g * 128:(g + 1) * 128], ident)
            t = T(f, k3) if g == 3 else T.quiet(f, k3)
        A(lambda: act.copy(catT[:, 8:12, tb * 128:(tb + 1) * 128],
                           PS[:, 2 + tb, :].rearrange("p (g q) -> p g q", g=4)), t)
    fence()

    O = ar.get(2048, "p (t e) -> p t e", t=2)
    pP = Slots([ar.get(1024, "p (m k) -> p m k", m=2) for _ in range(3)])
    pA = Slots([ar.get(512) for _ in range(2)])
    pT = Slots([ar.get(512) for _ in range(2)])
    sB = Slots([0, 1, 2, 3])
    tB = Slots([4, 5])
    oB = Slots([6, 7])
    stt = Slots([SM[:, 36 + 8 * i:44 + 8 * i] for i in range(3)])
    units = [(h, qb) for h in range(8) for qb in range(2)]
    live = {}

    def scores(u):
        h, qb = units[u]
        pi, P, pf = pP.take()
        si, s8, sf = stt.take()
        ks = []
        for m in range(2):
            bi, bk, fr = sB.take()
            t = mm(PS[:, bk, :], qT[64 * m:64 * m + 64, h, qb * 128:(qb + 1) * 128], kT[64 * m:64 * m + 64, h, :],
                   True, True, *fr, inc=True)
            k1 = V(lambda: vec.tensor_reduce(s8[:, m:m + 1], PS[:, bk, :], AX, ALU.max), t, *sf)
            k1 = V(lambda: vec.tensor_scalar(s8[:, 2 + m:3 + m], s8[:, m:m + 1], -0.125, None, ALU.mult), k1)
            k1 = A(lambda: act.activation(P[:, m, :], PS[:, bk, :], ACT.Exp, bias=s8[:, 2 + m:3 + m], scale=0.125,
                                          accum_out=s8[:, 4 + m:5 + m]), k1, *pf)
            sB.done(bi, k1)
            ks.append(k1)
        live[u] = (pi, P, si, s8, ks)

    def combine(u):
        pi, P, si, s8, ks = live[u]
        ai, Am, af = pA.take()
        k1 = V(lambda: vec.reciprocal(s8[:, 6:8], s8[:, 4:6]), *ks)
        k2 = V(lambda: vec.tensor_tensor(s8[:, 7:8], s8[:, 7:8], lam[:, 3:4], ALU.mult), k1, k_lam)
        k3 = V(lambda: vec.tensor_scalar(P[:, 1, :], P[:, 1, :], s8[:, 7:8], None, ALU.mult), k2)
        k4 = V(lambda: vec.scalar_tensor_tensor(Am, P[:, 0, :], s8[:, 6:7], P[:, 1, :], ALU.mult, ALU.add), k3, *af)
        pP.done(pi, k4)
        stt.done(si, k4)
        live[u] = (ai, Am, k4)

    def turn(u):
        ai, Am, k4 = live[u]
        bi, bk, fr = tB.take()
        ti, At, tf = pT.take()
        T.wait(k4, *fr)
        for j in range(4):
            f = lambda: tns.transpose(PS[:, bk, j * 128:(j + 1) * 128], Am[:, j * 128:(j + 1) * 128], ident)
            t = T(f) if j == 3 else T.quiet(f)
        pA.done(ai, t)
        k5 = A(lambda: act.copy(At, PS[:, bk, :]), t, *tf)
        tB.done(bi, k5)
        live[u] = (ti, At, k5)

    def values(u):
        h, qb = units[u]
        ti, At, k5 = live[u]
        bi, bk, fr = oB.take()
        T.wait(k5, *fr)
        for j in range(4):
            t = mm(PS[:, bk, 0:128], At[:, j * 128:(j + 1) * 128], va[:, j, h * 128:(h + 1) * 128], j == 0, j == 3,
                   inc=(j == 3))
        pT.done(ti, t)
        oB.done(bi, V(lambda: vec.tensor_copy(O[:, qb, h * 128:(h + 1) * 128], PS[:, bk, 0:128]), t))

    for s in range(len(units) + 3):
        for stage, lag in ((scores, 0), (combine, 1), (turn, 2), (values, 3)):
            if 0 <= s - lag < len(units):
                stage(s - lag)
    fence()

    def head_norm(O, gain, scale, eps, k=None):
        o3 = O.rearrange("p t (h e) -> p (t h) e", e=128)
        t3 = TMP[:, :].rearrange("p (n e) -> p n e", e=128)
        r = SM[:, 0:16]
        k1 = V(lambda: vec.tensor_tensor(t3, o3, o3, ALU.mult), k)
        k1 = V(lambda: vec.tensor_reduce(r, t3, AX, ALU.add), k1)
        k1 = V(lambda: vec.tensor_scalar(r, r, 1.0 / 128, eps, ALU.mult, ALU.add), k1)
        k1 = A(lambda: act.sqrt(r, r), k1)
        k1 = V(lambda: vec.reciprocal(r, r), k1)
        k1 = V(lambda: vec.tensor_tensor(t3, o3, r.unsqueeze(2).to_broadcast([128, 16, 128]), ALU.mult), k1)
        g3 = gain.unsqueeze(1).to_broadcast([128, 16, 128])
        k1 = V(lambda: vec.tensor_tensor(o3, t3, g3, ALU.mult), k1)
        if scale != 1.0:
            k1 = V(lambda: vec.tensor_scalar(o3, o3, scale, None, ALU.mult), k1)
        return k1

    k1 = head_norm(O, row("dng"), 1.0 - lam_init, 1e-5)

    def rows_to_T(src, dst, n, banks, k):
        b4 = Slots(banks)
        for q in range(n // 2):
            bi, bk, fr = b4.take()
            T.wait(k, *fr)
            for j in range(4):
                c, tb = 2 * q + j // 2, j % 2
                f = lambda: tns.transpose(PS[:, bk, j * 128:(j + 1) * 128], src[:, tb, c * 128:(c + 1) * 128], ident)
                t = T(f) if j == 3 else T.quiet(f)
            o = dst[:, 2 * q:2 * q + 2, :].rearrange("p c t -> p (c t)")
            e = A(lambda: act.copy(o, PS[:, bk, :]), t)
            b4.done(bi, e)
        return e

    k1 = rows_to_T(O, catT[:, 0:8, :], 8, [4, 5, 6, 7], k1)
    kg = gate_rows(mod0[:, 16:24], [6, 7], k_mod0, (k1,))
    YB = [[0, 1], [2, 3]]
    k_y = rows_out("about", catT, 12, YB, (k1,))
    V.wait(k_x)
    residual_ln(0, k_ln, YB, k_y, kg)

    if dbg is not None and upto == 0:
        s = sem("dbg")
        S.wait(V.now())
        syn.dma_start(dbg.rearrange("(t p) d -> p t d", p=128), xs).then_inc(s, 16)
        syn.wait_ge(s, 16)
        return

    def peer(layer, sc, sh, gate_cols, extra):
        ar = Arena()
        sp = Splitter(ar)
        HH, HL = (ar.get(2048, "p (c t) -> p c t", dt=R, c=8) for _ in range(2))
        Wt = ar.get(16384)
        i1T, i2T = ar.get(256), ar.get(256)
        gT = ar.get(512, "p (c t) -> p c t", dt=F16, c=2)
        CHs = Slots([(ar.get(256, dt=R), ar.get(256, dt=R)) for _ in range(2)])
        more = [ar.get(256) for _ in range(LEAD - 12)]
        kc_ = Wt[:, 0:2048]
        kys = kc_.rearrange("p (h n) -> p h n", h=16)
        kn, kslot, kk = weight(f"keys{layer}", 0)
        sp.start(f"wq{layer}", 1)
        make_hT(sc, sh, HH, HL)
        kk = A(lambda: act.copy(kc_, kslot), kk)
        release(kn, kk)
        T.wait(kk)
        u_s, v_s = Slots([0, 1024, 2048, 3072]), Slots([2048, 3072])
        ub = Slots([6, 7])
        order = ([GR[:, 256 * i:256 * i + 256] for i in range(4)] + [LN[:, 256 * i:256 * i + 256] for i in range(8)]
                 + more + [HT[:, 512 + 256 * i:768 + 256 * i] for i in range(2)])
        Gs = Slots([order[(i - (128 - LEAD)) % len(order)] for i in range(len(order))])
        ups, lead, downs, y_done = {}, {}, {}, {}

        def split_up(s, src, k, eng=None):
            ui, at_, fr = u_s.take()
            hi, lo, b = sp.part(at_, 1024, src, k, *fr, eng=eng)
            ups[s] = (ui, hi, lo, b)
            return b

        def up(s):
            ui, hi, lo, b = ups.pop(s)
            h3, l3 = (z.rearrange("p (c e) -> p c e", c=8) for z in (hi, lo))
            bi, bk, fr = ub.take()
            T.wait(b, *fr)
            for c in range(8):
                t = mm3(PS[:, bk, 0:256], (h3[:, c, :], l3[:, c, :]), (HH[:, c, :], HL[:, c, :]), c == 0, c == 7)
            u_s.done(ui, t)
            gi, Gt, gf_ = Gs.take()
            k1 = A(lambda: act.activation(Gt, PS[:, bk, 0:256], ACT.Gelu_apprx_tanh), t, *gf_)
            ub.done(bi, k1)
            lead[s] = (gi, Gt, k1)

        ahead = [0]

        def next_up():
            s = ahead[0]
            if s < LEAD:
                if s % 2 == 0:
                    pair[:] = weight(f"up{layer}", s // 2)
                b = split_up(s, pair[1][:, s % 2 * 1024:s % 2 * 1024 + 1024], pair[2], eng=G)
                if s % 2:
                    release(pair[0], b)
            if 2 <= s < LEAD + 2:
                up(s - 2)
            ahead[0] = s + 1

        pair = []

        def more_ups(n):
            for _ in range(n):
                next_up()

        at = [2048]

        def tp(n):
            at[0] += n
            return Wt[:, at[0] - n:at[0]]

        qS = Slots([tp(512) for _ in range(2)])
        sS = Slots([(tp(512), tp(512)) for _ in range(2)])
        cS = Slots([(tp(512), tp(512)) for _ in range(2)])
        tS = Slots([(tp(64), tp(64), tp(64), tp(32), tp(64), tp(64)) for _ in range(2)])
        eS = Slots([tp(1024) for _ in range(2)])
        BS, E, x1, x2, gf = tp(256), tp(256), tp(256), tp(256), tp(256)
        rr = tp(16)
        BIG = -3.0e38
        qB, kB = Slots([0, 1, 2, 3]), Slots([4, 5])
        def top16(vals, idx, src, work, width, ready):
            n = len(vals)
            rows = [(vals[r], idx[r], src[:, r * width:(r + 1) * width], work[:, r * width:(r + 1) * width])
                    for r in range(n)]
            a = [V(lambda: vec.max(v[:, 0:8], s), ready) for v, i, s, z in rows]
            b = [V(lambda: vec.match_replace(z, v[:, 0:8], s, BIG), a[r]) for r, (v, i, s, z) in enumerate(rows)]
            for v, i, s, z in rows:
                V(lambda: vec.max_index(i[:, 0:8], v[:, 0:8], s))
            c = [V(lambda: vec.max(v[:, 8:16], z), b[r]) for r, (v, i, s, z) in enumerate(rows)]
            for r, (v, i, s, z) in enumerate(rows):
                d = V(lambda: vec.max_index(i[:, 8:16], v[:, 8:16], z), c[r])
            return d

        def route(h, hi, lo):
            qi, q, qf = qS.take()
            kq = []
            for b in range(2):
                bi, bk, fr = qB.take()
                T.wait(*fr)
                t_last = projT3(hi, lo, b, HH, HL, PS[:, bk, 0:256])
                kq.append(A(lambda: act.copy(q[:, b * 256:(b + 1) * 256], PS[:, bk, 0:256]), t_last, *qf))
                qB.done(bi, kq[-1])
            bi, bk, fr = kB.take()
            T.wait(*kq, *fr)
            for tb in range(2):
                for p in range(2):
                    t = mm(PS[:, bk, (tb * 2 + p) * 128:(tb * 2 + p + 1) * 128],
                           q[:, p * 256 + tb * 128:p * 256 + tb * 128 + 128], kys[:, 2 * h + p, :], True, True,
                           inc=(tb == 1 and p == 1))
            qS.done(qi, t)
            si, (S1, S2), sf = sS.take()
            k = A(lambda: act.copy(S1, PS[:, bk, :]), t, *sf)
            kB.done(bi, k)
            ti, (TSh, TIh, TIf, BPh, PU, PF), tf = tS.take()
            V.wait(*tf)
            r4 = lambda z: [z[:, 16 * r:16 * r + 16] for r in range(4)]
            kd = top16(r4(TSh), r4(TIh.bitcast(U32)), S1, S2, 128, k)
            sS.done(si, kd)
            ci, (c1, c2), cf = cS.take()
            t4 = TSh.rearrange("p (t s k) -> p t s k", t=2, s=2)
            cand = c1.rearrange("p (t a b) -> p t a b", t=2, a=16)
            kc = V(lambda: vec.tensor_tensor(cand, t4[:, :, 0, :].unsqueeze(3).to_broadcast([128, 2, 16, 16]),
                                             t4[:, :, 1, :].unsqueeze(2).to_broadcast([128, 2, 16, 16]), ALU.add),
                   kd, *cf)
            k3 = V(lambda: vec.tensor_copy(TIf, TIh.bitcast(U32)), kd)
            o = h * 16
            kb = top16([BS[:, tb * 128 + o:tb * 128 + o + 16] for tb in range(2)],
                       [BPh[:, tb * 16:tb * 16 + 16].bitcast(U32) for tb in range(2)], c1, c2, 256, kc)
            cS.done(ci, kb)
            pu, bp = PU.bitcast(U32), BPh.bitcast(U32)
            k1 = V(lambda: vec.tensor_scalar(pu[:, 0:32], bp, 4, None, ALU.logical_shift_right), kb)
            k2 = V(lambda: vec.tensor_scalar(pu[:, 32:64], bp, 15, None, ALU.bitwise_and), kb)
            k4 = V(lambda: vec.tensor_copy(PF, pu), k2)
            ei, eq, ef = eS.take()
            k5 = V(lambda: vec.tensor_tensor(eq.rearrange("p (n a) -> p n a", a=16),
                                             iota16.unsqueeze(1).to_broadcast([128, 64, 16]),
                                             PF.unsqueeze(2).to_broadcast([128, 64, 16]), ALU.is_equal), k3, k4, *ef)
            f4 = TIf.rearrange("p (t s a) -> p t s a", t=2, s=2)
            for s in range(2):
                es = eq[:, s * 512:(s + 1) * 512].rearrange("p (t k a) -> p t k a", t=2, k=16)
                k6 = G(lambda: gps.tensor_tensor(es, es, f4[:, :, s, :].unsqueeze(2).to_broadcast([128, 2, 16, 16]),
                                                 ALU.mult), k5)
            tS.done(ti, k6, kb)
            pending.append((h, ei, eq, k6))
            return t_last

        def finish(h, ei, eq, k6):
            for s, dst in enumerate((x1, x2)):
                es = eq[:, s * 512:(s + 1) * 512].rearrange("p (t k a) -> p t k a", t=2, k=16)
                d3 = dst.rearrange("p (t h k) -> p t h k", t=2, h=8)[:, :, h, :]
                k = V(lambda: vec.tensor_reduce(d3, es, AX, ALU.add), k6)
            eS.done(ei, k)
            return k

        pending = []

        def body(n, hi, lo):
            if n == 7:
                for i in range(2):
                    u_s.done(i, *sp.slots.free[0])
                more_ups(2)
            t = route(n, hi, lo)
            if n == 7:
                for i in range(2, 4):
                    u_s.done(i, t)
                more_ups(2)
            if n:
                finish(*pending.pop(0))
            return t

        sp.run(f"wq{layer}", list(range(8)), body, G)
        last = finish(*pending.pop(0))
        b3 = BS.rearrange("p (n k) -> p n k", k=16)
        e3 = E.rearrange("p (n k) -> p n k", k=16)
        k1 = V(lambda: vec.tensor_tensor(e3, b3, b3[:, :, 0:1].to_broadcast([128, 16, 16]), ALU.subtract), V.now())
        k_e = A(lambda: act.activation(E, E, ACT.Exp), k1)
        k6 = V(lambda: vec.tensor_reduce(rr, e3, AX, ALU.add), k_e)
        k6 = V(lambda: vec.reciprocal(rr, rr), k6)
        k6 = V(lambda: vec.tensor_scalar(rr, rr, GSCALE, None, ALU.mult), k6)
        k6 = V(lambda: vec.tensor_tensor(e3, e3, rr.unsqueeze(2).to_broadcast([128, 16, 16]), ALU.mult), k6)
        for n, (src, dst) in enumerate(((x1, i1T), (x2, i2T), (E, gf))):
            for tb in range(2):
                t = T(lambda: tns.transpose(PS[:, n, tb * 128:(tb + 1) * 128], src[:, tb * 128:(tb + 1) * 128],
                                            ident), last, k6, A.now())
            k7 = A(lambda: act.copy(dst, PS[:, n, 0:256]), t)
        k8 = A(lambda: act.copy(gT[:, 0, :], gf), k7)
        k_g = V(lambda: vec.tensor_tensor(gT[:, 1, :], gf, gT[:, 0, :], ALU.subtract), k8)
        more_ups(2)
        for e in (V, A, G):
            e.wait(k7, k_g)

        Wq = [Wt[:, 8192 * b:8192 * b + 8192].rearrange("p (j t) -> p j t", j=PW) for b in range(2)]
        h16 = lambda a, n: TMP[:, a:a + n // 2].bitcast(F16)
        As = Slots([z.rearrange("p (t m) -> p t m", t=GT)
                    for z in (h16(0, 1024), h16(512, 1024), Wt[:, 8192:8704].bitcast(F16), Wt[:, 8704:9216].bitcast(F16))])
        Os = Slots([h16(1024 + 128 * i, 256).rearrange("p (t j) -> p t j", t=GT) for i in range(2)])
        Bs = Slots([z.rearrange("p (t c j) -> p t c j", t=GT, c=2)
                    for z in (h16(1280, 512), h16(1536, 512), Wt[:, 9216:9472].bitcast(F16), Wt[:, 9472:9728].bitcast(F16))])
        Cs = Slots([HT[:, 256 * i:256 * i + 256] for i in range(2)])
        iota_h = h16(1792, 128)
        k_i = V(lambda: vec.tensor_copy(iota_h, iota))
        V.wait(k_i)
        A.wait(k_i)
        wb = Slots([4, 5])
        w_done, c_done = {}, {}

        def make_onehots(part, g, eng):
            toks = slice(g * GT, (g + 1) * GT)
            ai, Am, af = As.take()
            oi, Om, of = Os.take()
            bi, Bm, bf = Bs.take()
            a3 = lambda z, n: z[:, toks].unsqueeze(2).to_broadcast([128, GT, n])
            io = lambda z, n: z.unsqueeze(1).to_broadcast([128, GT, n])
            if eng is G:
                for r in range(GT):
                    tok = g * GT + r
                    ka = G(lambda: gps.tensor_scalar(Am[:, r, :], iota_h, i1T[:, tok:tok + 1], None, ALU.is_equal), *af)
            elif eng is A:
                for r in range(GT):
                    tok = g * GT + r
                    ka = A(lambda: act.activation(Am[:, r, :], iota_h, ACT.Abs, bias=i1T[:, tok:tok + 1], scale=-1.0),
                           *af)
                ka = A(lambda: act.activation(Am, Am, ACT.Relu, bias=1.0, scale=-1.0), ka)
            else:
                for r in range(GT):
                    tok = g * GT + r
                    ka = V(lambda: vec.tensor_scalar(Am[:, r, :], iota_h, i1T[:, tok:tok + 1], None, ALU.is_equal),
                           *af)
            ko = V(lambda: vec.tensor_tensor(Om, io(iota[:, part * PW:(part + 1) * PW], PW), a3(i2T, PW),
                                             ALU.is_equal), *of)
            g2 = gT[:, :, toks].rearrange("p c t -> p t c").unsqueeze(3).to_broadcast([128, GT, 2, PW])
            kb = V(lambda: vec.tensor_tensor(Bm, Om.unsqueeze(2).to_broadcast([128, GT, 2, PW]), g2, ALU.mult), ko,
                   *bf)
            Os.done(oi, kb)
            return part, g, ai, Am, bi, Bm, ka, kb

        def add_gates(part, g, ai, Am, bi, Bm, ka, kb):
            wi, bk, fr = wb.take()
            T.wait(ka, kb, *fr)
            for r in range(GT):
                o = PS[:, bk, r * PW:(r + 1) * PW]
                mm(o, Am[:, r, :], Bm[:, r, 0, :], True, False)
                t = mm(o, Am[:, r, :], Bm[:, r, 1, :], False, True, inc=(r == GT - 1))
            As.done(ai, t)
            Bs.done(bi, t)
            k = A(lambda: act.copy(Wq[part % 2][:, :, g * GT:(g + 1) * GT],
                                   PS[:, bk, 0:GT * PW].rearrange("p (t j) -> p j t", j=PW)), t,
                  c_done.get(part - 2))
            wb.done(wi, k)
            w_done[part] = k

        def split_down(s, src, k, eng=None):
            vi, at_, fr = v_s.take()
            hi, lo, b = sp.part(at_, 1024, src, k, *fr, eng=eng)
            downs[s] = [vi, hi, lo, b]
            return b

        def gated(s):
            gi, Gt, k1 = lead.pop(s)
            part, j = s // PW, s % PW
            ci, Ct, cf = Cs.take()
            hi_, (Ch, Cl), hf = CHs.take()
            k2 = V(lambda: vec.scalar_tensor_tensor(Ct, Gt, 1.0 / GSCALE, Wq[part % 2][:, j, :], ALU.mult, ALU.mult),
                   k1, w_done[part], *cf)
            c_done[part] = k2
            Gs.done(gi, k2)
            k3 = A(lambda: act.copy(Ch, Ct), k2, *hf)
            k4 = V(lambda: vec.tensor_tensor(Cl, Ct, Ch.bitcast(F), ALU.subtract), k3, *hf)
            Cs.done(ci, k4)
            downs[s] += [hi_, Ch, Cl, k4]

        def down(s):
            vi, hi, lo, b, hi_, Ch, Cl, k4 = downs.pop(s)
            T.wait(k4, b)
            for tb in range(2):
                sl = slice(tb * 128, (tb + 1) * 128)
                for a, z in ((Ch, hi), (Ch, lo), (Cl, hi)):
                    for nh in range(2):
                        t = mm(PS[:, YB[tb][nh], :], a[:, sl], z[:, nh * 512:(nh + 1) * 512],
                               s == 0 and a is Ch and z is hi, s == 127 and a is Cl,
                               inc=(nh == 1 and a is Cl))
                y_done[tb] = t
            v_s.done(vi, t)
            CHs.done(hi_, t)
            return t

        V.wait(k_g)
        prev = []
        for g in range(256 // GT):
            cur = make_onehots(0, g, A if g % 4 == 2 else (G if g in (5, 13, 21, 25, 29) else V))
            prev.append(cur)
            if len(prev) > 3:
                add_gates(*prev.pop(0))
            if g % 2 == 1 or g < 6:
                more_ups(1)
        for z in prev:
            add_gates(*z)
        more_ups(max(LEAD + 2 - ahead[0], 0))
        for z in (As, Bs):
            z.items = z.items[0:2]
            for i in (0, 1):
                z.done(i, T.now())
        u_s.items = [0, 1024]
        u_s.n = 0
        for i in range(2):
            u_s.done(i, T.now())
            v_s.done(i, T.now())
        prev = make_onehots(1, 0, G)

        def begin(s):
            held[s] = weight(f"uv{layer}", s)
            split_up(s + LEAD, held[s][1][:, 0:1024], held[s][2])
            if s % 4 == 3 and extra:
                extra.pop(0)()

        def last_split(m):
            if m < LEAD:
                if m % 2 == 0:
                    pair[:] = weight(f"down{layer}", m // 2)
                b = split_down(128 - LEAD + m, pair[1][:, m % 2 * 1024:m % 2 * 1024 + 1024], pair[2], eng=G)
                if m % 2:
                    release(pair[0], b)

        held = {}
        begin(0)
        for s in range(128):
            if s < 128 - LEAD:
                if s + 1 < 128 - LEAD:
                    begin(s + 1)
                n, slot, k = held.pop(s)
                release(n, split_down(s, slot[:, 1024:2048], k))
                up(s + LEAD)
            else:
                if s == 128 - LEAD:
                    i = v_s.n % 2
                    v_s.items = [v_s.items[i], 0, 1024, v_s.items[1 - i]]
                    v_s.free = {0: v_s.free[i], 1: (T.now(),), 2: (T.now(),), 3: ()}
                    v_s.n = 0
                    last_split(0)
                    last_split(1)
                gated(s)
                last_split(s + 2 - (128 - LEAD))
            part, g = s // PW + 1, s % PW
            if part < NPART:
                nxt = (part, g + 1) if g + 1 < PW else (part + 1, 0)
                nx = make_onehots(*nxt, G) if nxt[0] < NPART else None
                add_gates(*prev)
                prev = nx
            if s < 128 - LEAD:
                gated(s)
            if s:
                t = down(s - 1)
                if s == 128 - LEAD:
                    v_s.done(3, t)
            if s == 128 - LEAD + 15:
                k_ln = load_ln(2 * layer + 1)
                kg = gate_rows(gate_cols, [6, 7], None, (T.now(), G.now(), A.now()))
        down(127)
        k_y = [((tb, nh), y_done[tb]) for tb in range(2) for nh in range(2)]
        assert not extra
        residual_ln(2 * layer + 1, k_ln, YB, k_y, kg)
        fence()
        ar.close()

    ar.close()
    fence()
    k_c2 = []

    def next_cond():
        ada_end(mod1, prm("ab1"), (8, 32))
        k_c2.append(fetch(CR[:, :], cnd_d[2].partition_broadcast(128), V.now()))

    def next_silu():
        k_c2.append(A(lambda: act.activation(CR[:, :], CR[:, :], ACT.Silu), k_c2.pop()))

    def mod2_end():
        for l in range(2):
            ada_end(mod2[l], prm(f"a2{l}"), (8,))

    peer(0, mod0[:, 32:40], mod0[:, 24:32], mod0[:, 40:48],
         [lambda n=n: ada("ada1", n, CR[:, :], mod1) for n in range(24)] + [next_cond, next_silu])

    def dump():
        s = sem("dbg")
        S.wait(V.now())
        syn.dma_start(dbg.rearrange("(t p) d -> p t d", p=128), xs).then_inc(s, 16)
        syn.wait_ge(s, 16)

    if dbg is not None and upto == 1:
        return dump()

    ar = Arena()
    sp = Splitter(ar)
    HH, HL = (ar.get(2048, "p (c t) -> p c t", dt=R, c=8) for _ in range(2))
    z = ar.get(2048, "p (t e) -> p t e", t=2)
    pm = ar.get(2048, "p (b g t) -> p b g t", b=2, g=4)
    k_pm = fetch(pm.rearrange("p b g t -> p (b g t)"), cst_d[:, CONST_AT["pool"][0]:CONST_AT["pool"][0] + 2048],
                 T.now(), V.now(), A.now())
    sp.start("pin", 1)
    make_hT(mod1[:, 8:16], mod1[:, 0:8], HH, HL)
    k_ln = load_ln(2)
    mT = ar.get(2048, "p (c t) -> p c t", c=8)
    eT = ar.get(2048, "p (c t) -> p c t", c=8)
    pb = Slots(range(8))

    def body(n, hi, lo):
        for tb in range(2):
            bi, bk, fr = pb.take()
            T.wait(*fr)
            t = projR3(hi, lo, tb, HH, HL, PS[:, bk, 0:256])
            pb.done(bi, A(lambda: act.copy(z[:, tb, n * 256:(n + 1) * 256], PS[:, bk, 0:256]), t))
        return t

    sp.run("pin", list(range(4)), body)
    kz = A.now()
    i, slot, k = weight("pgrp", 0)
    sp.start("pout", 1)
    kg = gate_rows(mod1[:, 16:24], [6, 7], None, (kz,))
    T.wait(kz, k_pm)
    for c in range(8):
        bi, bk, fr = pb.take()
        T.wait(*fr, *([kg] if c == 6 else []))
        for b in range(2):
            t = mm(PS[:, bk, 0:256], z[:, b, c * 128:(c + 1) * 128], pm[:, b, c // 2, :], b == 0, b == 1, inc=(b == 1))
        k1 = A(lambda: act.copy(mT[:, c, :], PS[:, bk, 0:256]), t)
        pb.done(bi, k1)
    wt = slot.rearrange("p (g c e) -> p g c e", g=4, c=2)
    T.wait(k1)
    for c in range(8):
        bi, bk, fr = pb.take()
        T.wait(*fr)
        for b in range(2):
            t = mm(PS[:, bk, 0:256], wt[:, c // 2, b, (c % 2) * 128:(c % 2 + 1) * 128], mT[:, 2 * (c // 2) + b, :],
                   b == 0, b == 1, k, inc=(b == 1))
        k1 = A(lambda: act.activation(eT[:, c, :], PS[:, bk, 0:256], ACT.Copy, scale=prm("psc")[:, c:c + 1]), t)
        pb.done(bi, k1)
        if c % 2:
            k2 = split_cols(eT, HH, HL, c - 1, c + 1, k1)
    release(i, t)
    k_y = rows_out3("pout", sp, HH, HL, YB, (kg, k2))
    residual_ln(2, k_ln, YB, k_y, kg)
    fence()
    ar.close()
    if dbg is not None and upto == 2:
        return dump()
    V.wait(*k_c2)
    peer(1, mod1[:, 32:40], mod1[:, 24:32], mod1[:, 40:48],
         [lambda n=n, l=l: ada(f"ad2{l}", n, CR[:, :], mod2[l]) for l in range(2) for n in range(12)] + [mod2_end])
    if dbg is not None and upto == 3:
        return dump()

    ar = Arena()
    sp = Splitter(ar, 3)
    HH, HL = (ar.get(2048, "p (c t) -> p c t", dt=R, c=8) for _ in range(2))
    sp.start("min", 1)
    make_hT(mod2[0][:, 8:16], mod2[0][:, 0:8], HH, HL)
    k_ln = load_ln(4)
    qT = ar.get(2048, "p (h t) -> p h t", h=8)
    kT = ar.get(2048, "p (h t) -> p h t", h=8)
    va = ar.get(2048, "p (b e) -> p b e", b=2)
    zT = ar.get(2048, "p (h t) -> p h t", h=8)
    oT = ar.get(2048, "p (h t) -> p h t", h=8)
    cm = ar.get(128)
    k_cm = fetch(cm, cst_d[:, CONST_AT["causal"][0]:CONST_AT["causal"][0] + 128], T.now(), V.now(), A.now())
    pb = Slots(range(6))
    gates = []

    def body(n, hi, lo):
        for b in range(2):
            bi, bk, fr = pb.take()
            T.wait(*fr)
            if 8 <= n < 12:
                t = projR3(hi, lo, b, HH, HL, PS[:, bk, 0:256])
                e = A(lambda: act.copy(va[:, b, (n - 8) * 256:(n - 7) * 256], PS[:, bk, 0:256]), t)
            else:
                t = projT3(hi, lo, b, HH, HL, PS[:, bk, 0:256])
                h = (2 * n + b) % 8
                if n < 8:
                    e = A(lambda: act.copy((qT if n < 4 else kT)[:, h, :], PS[:, bk, 0:256]), t)
                else:
                    e = A(lambda: act.activation(zT[:, h, :], PS[:, bk, 0:256], ACT.Silu), t)
            pb.done(bi, e)
        if n == 8:
            gates.append(gate_rows(mod2[0][:, 16:24], [6, 7], None))
        return t

    sp.run("min", list(range(16)), body)
    fence()
    V.wait(k_cm)
    SC2 = 128.0 ** -0.5
    sS = Slots([ar.get(256) for _ in range(3)])
    pT = Slots([ar.get(384) for _ in range(2)])
    sB, tB, oB = Slots([0, 1, 2]), Slots([3, 4, 5]), Slots([6, 7])
    stt = Slots([SM[:, 8 * i:8 * i + 4] for i in range(4)])
    units = [(h, qb) for h in range(8) for qb in range(2)]

    split = []

    def scores2(u):
        h, qb = units[u]
        nk = 128 * (qb + 1)
        si, Sm, sf = sS.take()
        ti, s4, tf = stt.take()
        bi, bk, fr = sB.take()
        t = mm(PS[:, bk, 0:nk], qT[:, h, qb * 128:(qb + 1) * 128], kT[:, h, 0:nk], True, True, *fr, inc=True)
        k1 = V(lambda: vec.tensor_tensor(Sm[:, nk - 128:nk], PS[:, bk, nk - 128:nk], cm, ALU.add), t, *sf)
        if qb:
            k1 = V(lambda: vec.tensor_copy(Sm[:, 0:128], PS[:, bk, 0:128]), t)
        sB.done(bi, k1)
        k1 = V(lambda: vec.tensor_reduce(s4[:, 0:1], Sm[:, 0:nk], AX, ALU.max), k1, V.now(), *tf)
        k1 = V(lambda: vec.tensor_scalar(s4[:, 1:2], s4[:, 0:1], -SC2, None, ALU.mult), k1)
        k1 = A(lambda: act.activation(Sm[:, 0:nk], Sm[:, 0:nk], ACT.Exp, bias=s4[:, 1:2], scale=SC2,
                                      accum_out=s4[:, 2:3]), k1)
        live[u] = (si, Sm, ti, s4, k1)

    def scale2(u):
        h, qb = units[u]
        nk = 128 * (qb + 1)
        si, Sm, ti, s4, k1 = live[u]
        k1 = V(lambda: vec.reciprocal(s4[:, 3:4], s4[:, 2:3]), k1)
        k1 = V(lambda: vec.tensor_scalar(Sm[:, 0:nk], Sm[:, 0:nk], s4[:, 3:4], None, ALU.mult), k1)
        stt.done(ti, k1)
        live[u] = (si, Sm, k1)

    def turn2(u):
        h, qb = units[u]
        si, Sm, k1 = live[u]
        bi, bk, fr = tB.take()
        T.wait(k1, *fr)
        for j in range(qb + 1):
            t = T(lambda: tns.transpose(PS[:, bk, j * 128:(j + 1) * 128], Sm[:, j * 128:(j + 1) * 128], ident))
        sS.done(si, t)
        ti, Pt, tf = pT.take()
        nk = 128 * (qb + 1)
        k2 = A(lambda: act.copy(Pt[:, 0:nk], PS[:, bk, 0:nk]), t, *tf)
        tB.done(bi, k2)
        live[u] = (ti, Pt, k2)

    def values2(u):
        h, qb = units[u]
        ti, Pt, k2 = live[u]
        bi, bk, fr = oB.take()
        T.wait(k2, *fr)
        for j in range(qb + 1):
            t = mm(PS[:, bk, 0:128], va[:, j, h * 128:(h + 1) * 128], Pt[:, j * 128:(j + 1) * 128], j == 0, j == qb,
                   inc=(j == qb))
        pT.done(ti, t)
        sl = slice(qb * 128, (qb + 1) * 128)
        k = V(lambda: vec.tensor_tensor(oT[:, h, sl], PS[:, bk, 0:128], zT[:, h, sl], ALU.mult), t)
        oB.done(bi, k)
        if h % 2 and qb:
            split.append(split_cols(oT, HH, HL, h - 1, h + 1, k))

    for s in range(len(units) + 3):
        for stage, lag in ((scores2, 0), (scale2, 1), (turn2, 2), (values2, 3)):
            if 0 <= s - lag < len(units):
                stage(s - lag)
        if s in (3, 7):
            sp.ready.append(sp.item("mout", len(sp.ready)))
    T.wait(V.now(), A.now())
    k_y = rows_out3("mout", sp, HH, HL, YB, (gates[0], split[-1]))
    residual_ln(4, k_ln, YB, k_y, gates[0])
    fence()
    ar.close()
    if dbg is not None and upto == 4:
        return dump()

    ar = Arena()
    Y = ar.get(6144, "p (n t) -> p n t", n=24)
    Z = ar.get(2048, "p (t e) -> p t e", t=2)
    gc0 = CONST_AT["utri"][0]
    GC = ar.get(CONST_AT["gdn_end"][0] - gc0)
    EG = ar.get(17)
    k_gc = fetch(GC, cst_d[:, gc0:CONST_AT["gdn_end"][0]], T.now(), V.now(), A.now())
    D = ar.get(2048, "p (n e) -> p n e", n=16)
    DT = ar.get(2048, "p (n e) -> p n e", n=16)
    ar2 = Arena()
    cvs = Slots([ar2.get(260)[:, 0:259] for _ in range(4)])
    sp = Splitter(ar2, 3)
    HH, HL = (ar2.get(2048, "p (c t) -> p c t", dt=R, c=8) for _ in range(2))
    i_gab, slot, k = weight("gab", 0)
    sp.start("gin", 1)
    make_hT(mod2[1][:, 8:16], mod2[1][:, 0:8], HH, HL)

    def gc(name):
        a, n = CONST_AT[name]
        return GC[:, a - gc0:a - gc0 + n]

    b4 = lambda bk: PS[:, bk, :].rearrange("p (n e) -> p n e", n=4)
    wt = slot[:, 0:128].rearrange("p (c f) -> p c f", c=8)
    for tb in range(2):
        t = projR(wt, hT, tb, PS[:, 7, tb * 16:tb * 16 + 16], k)
    release(i_gab, t)
    xa, ga, be, gcm = SM[:, 0:16], SM[:, 16:32], SM[:, 32:48], SM[:, 48:64]
    sp1, sp2 = TMP[:, 16:32], TMP[:, 32:48]
    ea = TMP[:, 48:56]
    ab = PS[:, 7, 0:32].rearrange("p (t s h) -> p t s h", t=2, s=2)
    c3 = lambda ap: ap.rearrange("p (t h) -> p t h", t=2)
    k1 = V(lambda: vec.tensor_tensor(c3(xa), ab[:, :, 0, :], row("dt").unsqueeze(1).to_broadcast([128, 2, 8]),
                                     ALU.add), t)
    k2 = A(lambda: act.activation(c3(be), ab[:, :, 1, :], ACT.Sigmoid), k1)
    k1 = V(lambda: vec.scalar_tensor_tensor(sp1, xa, -1.0, xa, ALU.mult, ALU.max), k1)
    k5 = A(lambda: act.activation(ea, row("alog"), ACT.Exp))
    k3 = A(lambda: act.activation(sp2, sp1, ACT.Exp, scale=-1.0), k1)
    k3 = A(lambda: act.activation(sp2, sp2, ACT.Ln, bias=1.0), k3)
    k4 = V(lambda: vec.tensor_scalar(xa, xa, 0.0, None, ALU.max), k1)
    k4 = V(lambda: vec.tensor_tensor(xa, xa, sp2, ALU.add), k3, k4)
    k4 = V(lambda: vec.tensor_tensor(c3(xa), c3(xa), ea.unsqueeze(1).to_broadcast([128, 2, 8]), ALU.mult), k4, k5)
    k_g = V(lambda: vec.tensor_scalar(ga, xa, -1.0, None, ALU.mult), k4, k2)
    gr = CR[:, :].rearrange("p (n e) -> p n e", n=8)
    GE = GR[:, :].rearrange("p (n e) -> p n e", n=8)
    glast = SM[:, 0:8]
    bgr = Slots([6, 7])

    def cumulate():
        t = mm(PS[:, 7, 0:16], gc("utri"), ga, True, True, k_gc, k_g, inc=True)
        V.wait(V(lambda: vec.tensor_copy(gcm, PS[:, 7, 0:16]), t), k_gc)

    def decay(c, hh):
        n0 = c * 8 + hh * 4
        g4 = gr[:, hh * 4:hh * 4 + 4, :]
        k1 = V(lambda: vec.tensor_copy(g4, ga[:, n0:n0 + 4].unsqueeze(2).to_broadcast([128, 4, 128])), T.now())
        bi, bk, fr = bgr.take()
        for h4 in range(4):
            t = mm(PS[:, bk, h4 * 128:(h4 + 1) * 128], gr[:, hh * 4 + h4, :], gc("utri"), True, True, k1, *fr,
                   inc=(h4 == 3))
        V.wait(t)
        for h4 in range(4):
            n = n0 + h4
            src = PS[:, bk, h4 * 128:(h4 + 1) * 128]
            V(lambda: vec.scalar_tensor_tensor(D[:, n, :], src, gcm[:, n:n + 1], gc("mD"), ALU.subtract, ALU.add))
            V(lambda: vec.scalar_tensor_tensor(DT[:, n, :], src, gcm[:, n:n + 1], gc("mDT"), ALU.subtract, ALU.add))
        if c == 0:
            k = V(lambda: vec.tensor_copy(glast[:, hh * 4:hh * 4 + 4], b4(bk)[:, :, 127]))
        else:
            k = V(lambda: vec.tensor_copy(GE[:, hh * 4:hh * 4 + 4, :], b4(bk)))
        bgr.done(bi, k)

    def exponentials():
        k1 = V(lambda: vec.tensor_tensor(EG[:, 0:8], glast, gcm[:, 0:8], ALU.subtract), V.now())
        A(lambda: act.activation(D, D, ACT.Exp, scale=-1.0), k1)
        A(lambda: act.activation(DT, DT, ACT.Exp))
        A(lambda: act.activation(GE, GE, ACT.Exp))
        A(lambda: act.activation(EG[:, 0:8], EG[:, 0:8], ACT.Exp))
        k1 = A(lambda: act.activation(EG[:, 8:16], gcm[:, 8:16], ACT.Exp))
        k1 = V(lambda: vec.tensor_tensor(EG[:, 8:16], be[:, 8:16], EG[:, 8:16], ALU.mult), k1)
        return V(lambda: vec.tensor_scalar(EG[:, 8:16], EG[:, 8:16], -1.0, None, ALU.mult), k1)

    eps = EG[:, 16:17]
    k_ep = V(lambda: vec.memset(eps, 1e-6))
    for c in cvs.items:
        k_z = V(lambda: vec.memset(c[:, 0:3], 0.0))
    cw = prm("conv").rearrange("p (n j) -> p n j", j=4)
    pb = Slots(range(6))
    q16 = Y[:, 0:16, :].rearrange("p n t -> p (n t)")
    sums = lambda n: (TMP, LN)[n // 4][:, n % 4 * 512:n % 4 * 512 + 512]
    convolved = []

    def activate():
        while convolved:
            y, k2 = convolved.pop(0)
            A(lambda: act.activation(y, y, ACT.Silu), k2)

    def squares_of(n):
        return A(lambda: act.activation(sums(n), q16[:, n * 512:n * 512 + 512], ACT.Square), A.now())

    def sum_squares(n, k):
        bi, bk, fr = pb.take()
        t = mm(PS[:, bk, :], ones, sums(n), True, True, k, *fr, inc=True)
        pb.done(bi, A(lambda: act.copy(sums(n), PS[:, bk, :]), t))

    def roots(z):
        return A(lambda: act.activation(z[:, :], z[:, :], ACT.Sqrt, bias=eps), A.now(), k_ep)

    def normalize(n, k):
        z, y = sums(n), q16[:, n * 512:n * 512 + 512]
        k = V(lambda: vec.reciprocal(z, z), k)
        return V(lambda: vec.scalar_tensor_tensor(y, y, 128.0 ** -0.5 if n < 4 else 1.0, z, ALU.mult, ALU.mult), k)

    k_rt = []
    turns_of = {7: 0, 8: 1, 10: 2, 11: 3, 12: 4, 13: 5, 14: 6, 15: 7}

    def body(n, hi, lo):
        activate()
        if 1 <= n < 9:
            k_sq = squares_of(n - 1)
        for b in range(2):
            bi, bk, fr = pb.take()
            T.wait(*fr)
            if n >= 12:
                t = projR3(hi, lo, b, HH, HL, PS[:, bk, 0:256])
                m = (n - 12) * 256
                pb.done(bi, A(lambda: act.activation(Z[:, b, m:m + 256], PS[:, bk, 0:256], ACT.Silu), t))
                continue
            nb = 2 * n + b
            t = projT3(hi, lo, b, HH, HL, PS[:, bk, 0:256])
            ci, cv, cf = cvs.take()
            k1 = A(lambda: act.copy(cv[:, 3:259], PS[:, bk, 0:256]), t, *cf)
            pb.done(bi, k1)
            if b and 1 <= n < 9:
                sum_squares(n - 1, k_sq)
            y = Y[:, nb, :]
            k2 = V(lambda: vec.tensor_scalar(y, cv[:, 3:259], cw[:, nb, 3:4], None, ALU.mult), k1, k_z)
            for j in (2, 1, 0):
                k2 = V(lambda: vec.scalar_tensor_tensor(y, cv[:, j:j + 256], cw[:, nb, j:j + 1], y, ALU.mult, ALU.add),
                       k2)
            cvs.done(ci, k2)
            convolved.append((y, k2))
        if n == 1:
            cumulate()
        if 2 <= n < 6:
            decay((n - 2) // 2, n % 2)
        if n == 6:
            exponentials()
            k_rt.append(roots(TMP))
        if n == 9:
            k_rt.append(roots(LN))
        if n in turns_of:
            normalize(turns_of[n], k_rt[turns_of[n] // 4])
        return t

    sp.run("gin", list(range(16)), body, lambda n: None if n in (0, 3, 6, 9, 12) else G)
    fence()
    ar2.close()
    k_ln = load_ln(5)
    Z3 = Z.rearrange("p t (h e) -> p (t h) e", e=128)
    k_zg = G(lambda: gps.tensor_tensor(Z3, Z3, row("nw").unsqueeze(1).to_broadcast([128, 16, 128]), ALU.mult))
    ar2, ar3 = Arena(), Arena()
    KN, VB, Ym = (ar2.get(2048, "p (n e) -> p n e", n=16) for _ in range(3))
    Lm = HT[:, :].rearrange("p (n e) -> p n e", n=16)
    TT = Y[:, 16:24, :].rearrange("p n t -> p (n t)").rearrange("p (n e) -> p n e", n=16)
    NT2, LT, Xm = (ar3.get(2048, "p (n e) -> p n e", n=16) for _ in range(3))
    NTs = [TMP[:, :].rearrange("p (n e) -> p n e", n=16), NT2]
    b16 = lambda ap, n=16: ap.unsqueeze(1).to_broadcast([128, n, 128])
    units = [(c, hh) for c in range(2) for hh in range(2)]
    psl, psr = Slots([4, 5, 6, 7]), Slots([0, 1, 2, 3])

    def rows_of(kind, dst):
        for c, hh in units:
            bi, bk, fr = psr.take()
            T.wait(*fr)
            for h4 in range(4):
                t = T(lambda: tns.transpose(PS[:, bk, h4 * 128:(h4 + 1) * 128],
                                            Y[:, 8 + 8 * kind + hh * 4 + h4, c * 128:(c + 1) * 128], ident))
            k = A(lambda: act.copy(dst[:, c * 8 + hh * 4:c * 8 + hh * 4 + 4, :], b4(bk)), t)
            psr.done(bi, k)
        return k

    for c, hh in units:
        bi, bk, fr = psl.take()
        T.wait(*fr)
        for h4 in range(4):
            kt = Y[:, 8 + hh * 4 + h4, c * 128:(c + 1) * 128]
            t = mm(PS[:, bk, h4 * 128:(h4 + 1) * 128], kt, kt, True, True, inc=(h4 == 3))
        for h4 in range(4):
            n = c * 8 + hh * 4 + h4
            kl = V(lambda: vec.scalar_tensor_tensor(Lm[:, n, :], PS[:, bk, h4 * 128:(h4 + 1) * 128],
                                                    be[:, n:n + 1], D[:, n, :], ALU.mult, ALU.mult), t)
        psl.done(bi, kl)
    kv = rows_of(1, VB)
    for c, hh in units:
        bi, bk, fr = psl.take()
        T.wait(kl, *fr)
        n0 = c * 8 + hh * 4
        for h4 in range(4):
            t = T(lambda: tns.transpose(PS[:, bk, h4 * 128:(h4 + 1) * 128], Lm[:, n0 + h4, :], ident))
        kt = A(lambda: act.copy(LT[:, n0:n0 + 4, :], b4(bk)), t)
        psl.done(bi, kt)
    kk = rows_of(0, KN)
    levels = (2, 4, 8, 16, 32, 64)
    k_x = V(lambda: vec.tensor_tensor(Xm, Lm, b16(gc("m1")), ALU.mult), kl)
    k_x = V(lambda: vec.tensor_tensor(Xm, b16(ident), Xm, ALU.subtract), k_x)
    k_n = V(lambda: vec.tensor_tensor(NTs[0], LT, b16(gc("mt2")), ALU.mult), kt)
    k_y0 = V(lambda: vec.tensor_tensor(Ym[:, 0:8, :], LT[:, 0:8, :], b16(gc("mt1"), 8), ALU.mult), kt)
    k_y0 = V(lambda: vec.tensor_tensor(Ym[:, 0:8, :], b16(ident, 8), Ym[:, 0:8, :], ALU.subtract), k_y0)
    k_y1 = G(lambda: gps.tensor_tensor(Ym[:, 8:16, :], LT[:, 8:16, :], b16(gc("mt1"), 8), ALU.mult), kt, k_gc)
    k_y1 = G(lambda: gps.tensor_tensor(Ym[:, 8:16, :], b16(ident, 8), Ym[:, 8:16, :], ALU.subtract), k_y1)
    c16 = lambda ap: ap.unsqueeze(2).to_broadcast([128, 16, 128])
    k_vb = G(lambda: gps.tensor_tensor(VB, VB, c16(be), ALU.mult), kv, V.now())
    k_kn = G(lambda: gps.tensor_tensor(KN, KN, c16(EG[:, 0:16]), ALU.mult), kk)
    ts = [k_x] * 4
    for li, b in enumerate(levels):
        NT = NTs[li % 2]
        kx, last = [], ts
        for q in range(4):
            for r in range(4):
                n = 4 * q + r
                t = mm(PS[:, q, r * 128:(r + 1) * 128], NT[:, n, :], Xm[:, n, :], True, True, k_n, last[q],
                       *((kk,) if li == 0 else ()), inc=(r == 3))
            kx.append(A(lambda: act.copy(TT[:, 4 * q:4 * q + 4, :], b4(q)), t))
        if b < 64:
            k_n = V(lambda: vec.tensor_tensor(NTs[(li + 1) % 2], LT, b16(gc(f"mt{levels[li + 1]}")), ALU.mult),
                    *last)
        if li == 0:
            T.wait(k_y0, k_y1, kt)
        ts = []
        for q in range(4):
            bx, by = 4 + q % 2, 6 + q % 2
            T.wait(kx[q], ts[q - 2] if q > 1 else last[2 + q])
            for r in range(4):
                n = 4 * q + r
                if b < 64:
                    mm(PS[:, bx, r * 128:(r + 1) * 128], Ym[:, n, :], TT[:, n, :], True, True)
            for r in range(4):
                n = 4 * q + r
                t = mm(PS[:, by, r * 128:(r + 1) * 128], TT[:, n, :], Ym[:, n, :], True, True, inc=(r == 3))
            sl = slice(4 * q, 4 * q + 4)
            if b < 64:
                V(lambda: vec.tensor_tensor(Xm[:, sl, :], Xm[:, sl, :], b4(bx), ALU.subtract), t)
            ts.append(V(lambda: vec.tensor_tensor(Ym[:, sl, :], Ym[:, sl, :], b4(by), ALU.subtract), t))
        if li == 0:
            for m, (c, hh) in enumerate(units):
                bk = 4 + m
                T.wait(ts[3])
                for h4 in range(4):
                    h = hh * 4 + h4
                    t = mm(PS[:, bk, h4 * 128:(h4 + 1) * 128], Y[:, 8 + h, c * 128:(c + 1) * 128],
                           Y[:, h, c * 128:(c + 1) * 128], True, True, inc=(h4 == 3))
                n0 = c * 8 + hh * 4
                V(lambda: vec.tensor_tensor(Lm[:, n0:n0 + 4, :], b4(bk), DT[:, n0:n0 + 4, :], ALU.mult), t)
            kq = V(lambda: vec.tensor_tensor(Y[:, 0:8, 128:256], Y[:, 0:8, 128:256], GE, ALU.mult), t, A.now())
            T.wait(kq)
    T.wait(*ts, k_vb, k_kn)
    V.wait(T.now(), A.now())
    A.wait(T.now(), V.now())
    G.wait(T.now(), V.now(), A.now())
    ar3.close()
    ar3 = Arena()
    sp = Splitter(ar3)
    HH, HL = (ar3.get(2048, "p (c t) -> p c t", dt=R, c=8) for _ in range(2))
    sp.start("gout", 1)
    NT = NTs[0]
    OS = VB
    ku, kw, ks = [], [], []
    for hh in range(2):
        for r in range(4):
            h = 4 * hh + r
            t = mm(PS[:, hh, r * 128:(r + 1) * 128], Ym[:, h, :], VB[:, h, :], True, True, inc=(r == 3))
        ku.append(A(lambda: act.copy(TT[:, 4 * hh:4 * hh + 4, :], b4(hh)), t))
        for r in range(4):
            h = 4 * hh + r
            t = mm(PS[:, 2 + hh, r * 128:(r + 1) * 128], KN[:, 8 + h, :], Ym[:, 8 + h, :], True, True, inc=(r == 3))
        kw.append(V(lambda: vec.tensor_copy(NT[:, 4 * hh:4 * hh + 4, :], b4(2 + hh)), t))
    for hh in range(2):
        T.wait(ku[hh])
        for r in range(4):
            h = 4 * hh + r
            t = mm(PS[:, 4 + hh, r * 128:(r + 1) * 128], KN[:, h, :], TT[:, h, :], True, True, inc=(r == 3))
        ks.append(A(lambda: act.copy(NT[:, 8 + 4 * hh:12 + 4 * hh, :], b4(4 + hh)), t))

    def output(c, hh, bk, *k):
        for r in range(4):
            n, h = 8 * c + 4 * hh + r, 4 * hh + r
            o = PS[:, bk, r * 128:(r + 1) * 128]
            t = mm(o, Lm[:, n, :], TT[:, n, :], True, c == 0, *k, inc=(c == 0 and r == 3))
            if c:
                t = mm(o, Y[:, h, 128:256], NT[:, 8 + h, :], False, True, inc=(r == 3))
        n0 = 8 * c + 4 * hh
        return A(lambda: act.copy(OS[:, n0:n0 + 4, :], b4(bk)), t)

    r16 = SM[:, 0:16]

    def normed(c, ko):
        cs = slice(8 * c, 8 * c + 8)
        o3, s3, r = OS[:, cs, :], Ym[:, cs, :], r16[:, cs]
        k = A(lambda: act.activation(s3, o3, ACT.Square), *ko, T.now())
        k = V(lambda: vec.tensor_reduce(r, s3, AX, ALU.add), k)
        k = V(lambda: vec.tensor_scalar(r, r, 1.0 / 128, 1e-6, ALU.mult, ALU.add), k)
        k = A(lambda: act.sqrt(r, r), k)
        k = V(lambda: vec.reciprocal(r, r), k)
        k = V(lambda: vec.tensor_tensor(o3, o3, r.unsqueeze(2).to_broadcast([128, 8, 128]), ALU.mult), k)
        return V(lambda: vec.tensor_tensor(o3, o3, Z3[:, cs, :], ALU.mult), k, k_zg)

    def turned(c, banks, ko):
        for hh, bk in enumerate(banks):
            T.wait(ko)
            for r in range(4):
                t = T(lambda: tns.transpose(PS[:, bk, r * 128:(r + 1) * 128], OS[:, 8 * c + 4 * hh + r, :], ident))
            dst = (slice(None), slice(4 * hh, 4 * hh + 4), slice(128 * c, 128 * c + 128))
            a = A(lambda: act.copy(HH[dst], b4(bk)), t)
            k = V(lambda: vec.tensor_tensor(HL[dst], b4(bk), HH[dst].bitcast(F), ALU.subtract), a)
        return a, k

    ko = [output(0, hh, 6 + hh) for hh in range(2)]
    ku = []
    for hh in range(2):
        T.wait(*ks, *kw)
        for r in range(4):
            h = 4 * hh + r
            mm(PS[:, hh, r * 128:(r + 1) * 128], Ym[:, 8 + h, :], VB[:, 8 + h, :], True, False)
            t = mm(PS[:, hh, r * 128:(r + 1) * 128], NT[:, h, :], NT[:, 8 + h, :], False, True, inc=(r == 3))
        ku.append(A(lambda: act.copy(TT[:, 8 + 4 * hh:12 + 4 * hh, :], b4(hh)), t))
    ko = normed(0, ko)
    ko1 = [output(1, hh, 2 + hh, ku[hh]) for hh in range(2)]
    kg = gate_rows(mod2[1][:, 16:24], [0, 1], None, (T.now(), *ku), CR)
    k_0 = turned(0, [4, 5], ko)
    ko1 = normed(1, ko1)
    k_1 = turned(1, [6, 7], ko1)
    k_y = rows_out3("gout", sp, HH, HL, YB, k_0, k_1)
    k1 = residual_ln(5, k_ln, YB, k_y, kg, turn=False)
    s = sem("out")
    S.wait(k1)
    syn.dma_start(out_d.rearrange("(t p) d -> p t d", p=128), xs).then_inc(s, 16)
    syn.wait_ge(s, 16)


def cols_items(wm, width=256):
    kk, n = wm.shape
    return wm.reshape(kk // 128, 128, n // width, width).transpose(2, 1, 0, 3).reshape(n // width, 128, -1)


def turned_items(wm):
    n = wm.shape[1]
    return wm.T.reshape(n // 256, 2, 128, 1024).transpose(0, 2, 1, 3).reshape(n // 256, 128, 2048)


def half_items(wm):
    kk = wm.shape[0]
    return wm.reshape(kk // 512, 4, 128, 2, 512).transpose(3, 0, 2, 1, 4).reshape(-1, 128, 2048)


def column(v):
    return v.reshape(-1, 128).T


def kernel(**a):
    import concourse.bacc as bacc
    from concourse.bass_utils import run_bass_kernel_spmd as run

    a = {k: np.asarray(v) for k, v in a.items()}
    nc = bacc.Bacc("TRN2", target_bir_lowering=False, num_devices=1)
    arrays, r = prepare(a, nc)
    nc_out = nc.dram_tensor("out", (256, 1024), F, kind="ExternalOutput").ap()
    build(nc, *r, nc_out)
    res = run(nc, [arrays], core_ids=[0])
    return res.results[0]["out"].reshape(1, 256, 1024)


def prepare(a, nc):
    arrays = {}

    def give(name, x):
        x = np.ascontiguousarray(x)
        arrays[name] = x
        return nc.dram_tensor(name, x.shape, F, kind="ExternalInput").ap()

    cst = constants()
    w = {}
    for l in range(2):
        w[f"ada{l}"] = give(f"w_ada{l}", turned_items(a["ada_w"][l]))
        w[f"ad2{l}"] = give(f"w_ad2{l}", turned_items(a["ada_w_2"][l]))
        w[f"wq{l}"] = give(f"w_wq{l}", cols_items(a["peer_wq"][l]))
        w[f"keys{l}"] = give(f"w_keys{l}", a["peer_keys"][l].reshape(16, 128, 128).transpose(2, 0, 1).reshape(1, 128, 2048))
        uv = np.empty((128, 128, 2, 1024), np.float32)
        uv[:, :, 0, :] = a["peer_u"][l].reshape(128, 128, 8, 128).transpose(1, 3, 2, 0).reshape(128, 128, 1024)
        uv[:, :, 1, :] = a["peer_v"][l].reshape(128, 128, 1024).transpose(1, 0, 2)
        w[f"uv{l}"] = give(f"w_uv{l}", np.concatenate([uv[LEAD:, :, 0], uv[:128 - LEAD, :, 1]], 2))
        two = lambda z: z.reshape(LEAD // 2, 2, 128, 1024).transpose(0, 2, 1, 3).reshape(LEAD // 2, 128, 2048)
        w[f"up{l}"] = give(f"w_up{l}", two(uv[:LEAD, :, 0]))
        w[f"down{l}"] = give(f"w_down{l}", two(uv[128 - LEAD:, :, 1]))
    w["abin"] = give("w_abin", cols_items(a["ab_w_in"][0]))
    w["about"] = give("w_about", half_items(a["ab_w_out"][0]))
    w["pin"] = give("w_pin", cols_items(a["pool_w_in"][0]))
    w["pgrp"] = give("w_pgrp", a["pool_w_grp"][0].reshape(4, 2, 128, 256).transpose(2, 0, 1, 3).reshape(1, 128, 2048))
    w["pout"] = give("w_pout", half_items(a["pool_w_out"][0]))
    w["min"] = give("w_min", cols_items(a["moba_w_in_2"][0]))
    w["mout"] = give("w_mout", half_items(a["moba_w_out_2"][0]))
    w["gin"] = give("w_gin", cols_items(a["gdn_w_in_2"][0][:, :4096]))
    w["gab"] = give("w_gab", cols_items(a["gdn_w_in_2"][0][:, 4096:], 16))
    w["gout"] = give("w_gout", half_items(a["gdn_w_out_2"][0]))
    prm = np.concatenate([
        column(a["ada_b"][0]), column(a["ada_b"][1]), column(a["ada_b_2"][0]), column(a["ada_b_2"][1]),
        a["sgu_b"][0].T, column(a["pool_scale"][0]),
        a["gdn_conv_w_2"][0].reshape(4, 24, 128).transpose(2, 1, 0).reshape(128, 96)], 1)
    rows = np.concatenate([
        a["diff_lam"][0].reshape(-1), a["diff_norm_g"][0], a["gdn_a_log_2"][0], a["gdn_dt_bias_2"][0],
        a["gdn_norm_w_2"][0], a["sgu_ln_g"][0], a["sgu_ln_b"][0]])
    lns = np.stack([v for l in range(2) for n in range(2) for v in (a["ln_g"][l, n], a["ln_b"][l, n])]
                   + [v for l in range(2) for v in (a["ln_g_2"][l], a["ln_b_2"][l])])
    r = (w, give("cst", cst), give("prm", prm), give("rows", rows),
         give("conds", np.stack([a["c"][0], a["c_ctx"], a["c_2"][0]])), give("x", a["x"][0]), give("xT", a["x"][0].T),
         give("cT", a["ctx"][0].T), give("sguw", a["sgu_w"][0].transpose(2, 0, 1).reshape(128, 512)),
         give("lns", lns))
    return arrays, r
```
